# Optimizing a Trainium2 kernel written in Bass

```python
import math
import jax, jax.numpy as jnp
from jax import lax
import numpy as np

D_MODEL = 1024
BATCH = 1
SEQ = 256
DEPTH = 2

N_MIXERS = 2
GRID_W = 64
S5_WIDTH = D_MODEL // 2
S5_GROUP = 16
S5_STATE = 64
S5_GROUPS = S5_WIDTH // S5_GROUP
DT_MIN = 1e-3
DT_MAX = 1e-1
N_HEADS = 16
HEAD_DIM = D_MODEL // N_HEADS
WIN_ROWS_MAX = 8
WIN_COLS = 16
Q_COL_BLOCK = 16
COL_BAND = Q_COL_BLOCK + WIN_COLS
N_COL_BLOCKS = GRID_W // Q_COL_BLOCK
N_GROUPS = 4
EXPERTS_PER_GROUP = 8
TOP_K_IN_GROUP = 2
EXPERT_FF = D_MODEL // 4
PLE_DIM = 256

N_S5_LAYERS = (DEPTH + 1) // 2
N_NAT_LAYERS = DEPTH // 2
RMS_EPS = 1e-6
MASK_VALUE = -1e30

kernel_name = "hybrid_s5_natten_hmoe_encoder"

def _rmsnorm(x, g):
    xf = x.astype(jnp.float32)
    y = xf * lax.rsqrt(jnp.mean(xf * xf, axis=-1, keepdims=True) + RMS_EPS)
    return (y * g.astype(jnp.float32)).astype(x.dtype)

def _ssm_combine(left, right):
    a_l, b_l = left
    a_r, b_r = right
    return a_r * a_l, a_r * b_l + b_r

def _s5_mixer(h, w_in, lam_re, lam_im, log_dt, b_re, b_im, c_re, c_im, d_skip, w_out):
    bsz, seq, _ = h.shape
    f32 = jnp.float32
    u = (h @ w_in).astype(f32)
    ug = u.reshape(bsz, seq, S5_GROUPS, S5_GROUP)
    y = d_skip.astype(f32) * u
    for direction, reverse in ((0, False), (1, True)):
        lam = lax.complex(lam_re[direction].astype(f32), lam_im[direction].astype(f32))
        dt = jnp.exp(log_dt[direction].astype(f32))[:, None]
        lam_bar = jnp.exp(lam * dt)
        b = lax.complex(b_re[direction].astype(f32), b_im[direction].astype(f32))
        c = lax.complex(c_re[direction].astype(f32), c_im[direction].astype(f32))
        b_bar = ((lam_bar - 1.0) / lam)[..., None] * b
        bu = jnp.einsum('gph,blgh->blgp', b_bar, ug)
        a = jnp.broadcast_to(lam_bar, bu.shape)
        _, states = lax.associative_scan(_ssm_combine, (a, bu), axis=1, reverse=reverse)
        y = y + jnp.einsum('ghp,blgp->blgh', c, states).real.reshape(bsz, seq, S5_WIDTH)
    act = jax.nn.gelu(y).astype(h.dtype)
    val, gate = jnp.split(act @ w_out, 2, axis=-1)
    return val * jax.nn.sigmoid(gate)

def _nat_mixer(h, w_qkv, q_norm, k_norm, rpb, w_o):
    bsz, seq, _ = h.shape
    rows = seq // GRID_W
    kh = min(WIN_ROWS_MAX, rows)
    qkv = (h @ w_qkv).reshape(bsz, seq, 3, N_HEADS, HEAD_DIM)
    q = _rmsnorm(qkv[:, :, 0], q_norm).astype(jnp.float32)
    k = _rmsnorm(qkv[:, :, 1], k_norm).astype(jnp.float32)
    v = qkv[:, :, 2]
    qg = q.reshape(bsz, rows, GRID_W, N_HEADS, HEAD_DIM)
    kg = k.reshape(bsz, rows, GRID_W, N_HEADS, HEAD_DIM)
    vg = v.reshape(bsz, rows, GRID_W, N_HEADS, HEAD_DIM)

    q_cols = np.arange(N_COL_BLOCKS)[:, None] * Q_COL_BLOCK + np.arange(Q_COL_BLOCK)[None, :]
    band_start = np.clip(np.arange(N_COL_BLOCKS) * Q_COL_BLOCK - WIN_COLS // 2, 0, GRID_W - COL_BAND)
    band_cols = band_start[:, None] + np.arange(COL_BAND)[None, :]
    win_start = np.clip(q_cols - WIN_COLS // 2, 0, GRID_W - WIN_COLS)
    rel_c = band_cols[:, None, :] - q_cols[:, :, None]
    col_mask = jnp.asarray((band_cols[:, None, :] >= win_start[:, :, None])
                           & (band_cols[:, None, :] < win_start[:, :, None] + WIN_COLS))
    col_idx = jnp.asarray(np.clip(rel_c + WIN_COLS - 1, 0, 2 * WIN_COLS - 2))
    band_cols_j = jnp.asarray(band_cols)
    rpb_f = rpb.astype(jnp.float32)
    scale = 1.0 / math.sqrt(HEAD_DIM)

    def row_fn(r):
        rs = jnp.clip(r - kh // 2, 0, rows - kh)
        q_row = lax.dynamic_index_in_dim(qg, r, axis=1, keepdims=False)
        q_blk = q_row.reshape(bsz, N_COL_BLOCKS, Q_COL_BLOCK, N_HEADS, HEAD_DIM)
        k_rows = lax.dynamic_slice_in_dim(kg, rs, kh, axis=1)
        v_rows = lax.dynamic_slice_in_dim(vg, rs, kh, axis=1)
        k_band = k_rows[:, :, band_cols_j]
        v_band = v_rows[:, :, band_cols_j]
        s = jnp.einsum('bjqhd,brjchd->bhjqrc', q_blk, k_band) * scale
        row_idx = rs + jnp.arange(kh) - r + (WIN_ROWS_MAX - 1)
        bias = rpb_f[:, row_idx][:, :, col_idx]
        s = s + jnp.transpose(bias, (0, 2, 3, 1, 4))[None]
        s = jnp.where(col_mask[None, None, :, :, None, :], s, MASK_VALUE)
        prob = jax.nn.softmax(s.reshape(s.shape[:4] + (kh * COL_BAND,)), axis=-1)
        prob = prob.reshape(s.shape).astype(v.dtype)
        o = jnp.einsum('bhjqrc,brjchd->bjqhd', prob, v_band)
        return o.reshape(bsz, GRID_W, N_HEADS, HEAD_DIM)

    out = lax.map(row_fn, jnp.arange(rows))
    out = jnp.moveaxis(out, 0, 1).reshape(bsz, seq, D_MODEL)
    return out @ w_o

def _hier_moe(h, w_group, b_group, w_expert, b_expert, w_gate, w_up, w_down):
    bsz, seq, d = h.shape
    t = h.reshape(bsz * seq, d)
    g_logits = (t @ w_group + b_group).astype(jnp.float32)
    g_prob = jax.nn.softmax(g_logits, axis=-1)
    g_val, g_idx = lax.top_k(g_prob, 1)
    e_logits = (t @ w_expert + b_expert).astype(jnp.float32).reshape(-1, N_GROUPS, EXPERTS_PER_GROUP)
    chosen = jnp.take_along_axis(e_logits, g_idx[:, :, None], axis=1)[:, 0]
    e_prob = jax.nn.softmax(chosen, axis=-1)
    e_val, e_idx = lax.top_k(e_prob, TOP_K_IN_GROUP)
    e_val = e_val / jnp.sum(e_val, axis=-1, keepdims=True)
    within = jnp.sum(jax.nn.one_hot(e_idx, EXPERTS_PER_GROUP, dtype=jnp.float32) * e_val[..., None], axis=1)
    combine = (jax.nn.one_hot(g_idx[:, 0], N_GROUPS, dtype=jnp.float32)[:, :, None]
               * g_val[:, :, None] * within[:, None, :]).astype(h.dtype)
    y = jnp.zeros_like(t)
    for g in range(N_GROUPS):
        a = jnp.einsum('td,edf->tef', t, w_gate[g])
        u = jnp.einsum('td,edf->tef', t, w_up[g])
        act = jax.nn.silu(a) * u * combine[:, g, :, None]
        y = y + jnp.einsum('tef,efd->td', act, w_down[g])
    return y.reshape(bsz, seq, d)

def setup_inputs(seed: int = 0) -> dict:
    key = jax.random.key(seed)
    ks = jax.random.split(key, 32)
    f32 = jnp.float32

    def nrm(k, shape, scale):
        return jax.random.normal(k, shape, f32) * scale

    n_idx = jnp.arange(S5_STATE, dtype=f32)
    s5_shape = (N_S5_LAYERS, 2, S5_GROUPS, S5_STATE)
    inp = {}
    inp["x"] = nrm(ks[0], (BATCH, SEQ, D_MODEL), 1.0)
    inp["p"] = nrm(ks[1], (DEPTH, BATCH, SEQ, PLE_DIM), 1.0)
    inp["norm_mix"] = 1.0 + nrm(ks[2], (DEPTH, D_MODEL), 0.01)
    inp["norm_ffn"] = 1.0 + nrm(ks[3], (DEPTH, D_MODEL), 0.01)
    inp["norm_ple"] = 1.0 + nrm(ks[4], (DEPTH, D_MODEL), 0.01)
    inp["s5_w_in"] = nrm(ks[5], (N_S5_LAYERS, D_MODEL, S5_WIDTH), D_MODEL ** -0.5)
    inp["s5_lam_re"] = -0.5 + nrm(ks[6], s5_shape, 0.01)
    inp["s5_lam_im"] = math.pi * n_idx + nrm(ks[7], s5_shape, 0.01)
    inp["s5_log_dt"] = jax.random.uniform(ks[8], (N_S5_LAYERS, 2, S5_GROUPS), f32,
                                          math.log(DT_MIN), math.log(DT_MAX))
    b_scale = (2.0 * S5_GROUP) ** -0.5
    inp["s5_b_re"] = nrm(ks[9], s5_shape + (S5_GROUP,), b_scale)
    inp["s5_b_im"] = nrm(ks[10], s5_shape + (S5_GROUP,), b_scale)
    c_shape = (N_S5_LAYERS, 2, S5_GROUPS, S5_GROUP, S5_STATE)
    inp["s5_c_re"] = nrm(ks[11], c_shape, 0.5 ** 0.5)
    inp["s5_c_im"] = nrm(ks[12], c_shape, 0.5 ** 0.5)
    inp["s5_d"] = nrm(ks[13], (N_S5_LAYERS, S5_WIDTH), 1.0)
    inp["s5_w_out"] = nrm(ks[14], (N_S5_LAYERS, S5_WIDTH, 2 * D_MODEL), S5_WIDTH ** -0.5)
    inp["nat_w_qkv"] = nrm(ks[15], (N_NAT_LAYERS, D_MODEL, 3 * D_MODEL), D_MODEL ** -0.5)
    inp["nat_q_norm"] = 1.0 + nrm(ks[16], (N_NAT_LAYERS, HEAD_DIM), 0.01)
    inp["nat_k_norm"] = 1.0 + nrm(ks[17], (N_NAT_LAYERS, HEAD_DIM), 0.01)
    inp["nat_rpb"] = nrm(ks[18], (N_NAT_LAYERS, N_HEADS, 2 * WIN_ROWS_MAX - 1, 2 * WIN_COLS - 1), 0.02)
    inp["nat_w_o"] = nrm(ks[19], (N_NAT_LAYERS, D_MODEL, D_MODEL), D_MODEL ** -0.5)
    inp["moe_w_group"] = nrm(ks[20], (DEPTH, D_MODEL, N_GROUPS), D_MODEL ** -0.5)
    inp["moe_b_group"] = nrm(ks[21], (DEPTH, N_GROUPS), 0.01)
    inp["moe_w_expert"] = nrm(ks[22], (DEPTH, D_MODEL, N_GROUPS * EXPERTS_PER_GROUP), D_MODEL ** -0.5)
    inp["moe_b_expert"] = nrm(ks[23], (DEPTH, N_GROUPS * EXPERTS_PER_GROUP), 0.01)
    e_shape = (DEPTH, N_GROUPS, EXPERTS_PER_GROUP)
    inp["moe_w_gate"] = nrm(ks[24], e_shape + (D_MODEL, EXPERT_FF), D_MODEL ** -0.5)
    inp["moe_w_up"] = nrm(ks[25], e_shape + (D_MODEL, EXPERT_FF), D_MODEL ** -0.5)
    inp["moe_w_down"] = nrm(ks[26], e_shape + (EXPERT_FF, D_MODEL), EXPERT_FF ** -0.5)
    inp["ple_w_proj"] = nrm(ks[27], (DEPTH, PLE_DIM, D_MODEL), PLE_DIM ** -0.5)
    inp["ple_w_gate"] = nrm(ks[28], (DEPTH, D_MODEL, D_MODEL), D_MODEL ** -0.5)
    return inp

def reference(x, p, norm_mix, norm_ffn, norm_ple,
              s5_w_in, s5_lam_re, s5_lam_im, s5_log_dt, s5_b_re, s5_b_im,
              s5_c_re, s5_c_im, s5_d, s5_w_out,
              nat_w_qkv, nat_q_norm, nat_k_norm, nat_rpb, nat_w_o,
              moe_w_group, moe_b_group, moe_w_expert, moe_b_expert,
              moe_w_gate, moe_w_up, moe_w_down,
              ple_w_proj, ple_w_gate):
    for i in range(DEPTH):
        j = i // N_MIXERS
        h = _rmsnorm(x, norm_mix[i])
        if i % N_MIXERS == 0:
            x = x + _s5_mixer(h, s5_w_in[j], s5_lam_re[j], s5_lam_im[j], s5_log_dt[j],
                              s5_b_re[j], s5_b_im[j], s5_c_re[j], s5_c_im[j],
                              s5_d[j], s5_w_out[j])
        else:
            x = x + _nat_mixer(h, nat_w_qkv[j], nat_q_norm[j], nat_k_norm[j],
                               nat_rpb[j], nat_w_o[j])
        h = _rmsnorm(x, norm_ffn[i])
        x = x + _hier_moe(h, moe_w_group[i], moe_b_group[i], moe_w_expert[i], moe_b_expert[i],
                          moe_w_gate[i], moe_w_up[i], moe_w_down[i])
        gate = jax.nn.sigmoid(_rmsnorm(x, norm_ple[i]) @ ple_w_gate[i])
        x = x + gate * (p[i] @ ple_w_proj[i])
    return x


_drawn_inputs = setup_inputs


def setup_inputs(seed=0):
    import zlib

    import numpy as np

    out = dict(_drawn_inputs(seed))
    spreads = {}
    factors = {'norm_ple': 8.0,
     's5_lam_re': 7.021,
     'nat_q_norm': 6.581,
     'nat_k_norm': 8.0,
     'nat_rpb': 28.957,
     'moe_b_group': 8.0,
     'moe_b_expert': 3.981}
    for name, (base, spread) in spreads.items():
        noise = np.random.default_rng([zlib.crc32(name.encode()), seed]).standard_normal(out[name].shape)
        drawn = base * np.exp(spread * noise) if base else spread * noise
        out[name] = __import__('jax').numpy.asarray(drawn.astype(out[name].dtype))
    for name, factor in factors.items():
        out[name] = (out[name] * factor).astype(out[name].dtype)
    return out
```

```python
import math
from contextlib import ExitStack

import concourse.bass as bass
from concourse import mybir

F32 = mybir.dt.float32
F32R = mybir.dt.float32r
U32 = mybir.dt.uint32
I32 = mybir.dt.int32
ALU = mybir.AluOpType
ACT = mybir.ActivationFunctionType
AX = mybir.AxisListType

P = 128
D = 1024
T = 256
TT = T // P
KD = D // P
EPS = 1e-6
SG, SH, SP_ = 32, 16, 64
SW = SG * SH
L = 8
NC_ = T // L
NH, HD, GW, ROWS = 16, 64, 64, 4
WR, WC = 8, 16
MASKV = -1e30
NG, EG = 4, 8
NE = NG * EG
FF = 256
CAP = 64
GE = 4
GS = GE * CAP
NSTEP = NE // GE
MAGIC = 12582912.0
TWO_PI_HI = 6.28125
TWO_PI_LO = 2 * math.pi - 6.28125
TURN = 6.2831850


def bc(ap, axis, n):
    dims = [list(d) for d in ap.ap]
    dims.insert(axis, [0, n])
    return bass.AP(ap.tensor, ap.offset, dims)


def program(nc, I, out):
    ctx = ExitStack()
    with ctx:
        sems = {}

        def S(name):
            if name not in sems:
                sems[name] = ctx.enter_context(nc.semaphore(name))
            return sems[name]

        base = 16512
        addr = [base]

        def at(name, shape, dtype, off):
            return nc.alloc_sbuf_tensor_at(name, shape, dtype, offset=off)

        def new(name, shape, dtype=F32):
            n = 4
            for s in shape[1:]:
                n *= s
            n = (n + 31) // 32 * 32
            t = at(name, shape, dtype, addr[0])
            addr[0] += n
            return t

        ident = new("ident", [P, P])
        tri = new("tri", [P, P])
        mhalf = new("mhalf", [P, 32])
        ones = new("ones", [P, P])
        iota_slot = new("iota_slot", [P, GS])
        iota_i = at("iota_i", [P, GS], I32, base + 160000)
        iota_e = new("iota_e", [P, NE])
        negh = new("negh", [P, 64])
        ss = new("ss", [P, 4])
        ms = new("ms", [P, 4])
        rstd = new("rstd", [P, 4])
        slot = new("slot", [P, 2, TT])
        wtok = new("wtok", [P, TT, NE])
        wslot = new("wslot", [P, 2, GE])
        many = new("many", [1, 1], I32)
        dskip = new("dskip", [P, SW // P])
        assert addr[0] <= base + 4096, addr[0] - base
        A0 = base + 4096
        x = at("x", [P, TT, D], F32, A0)
        A_H = A0 + 8192
        hhi = at("hhi", [P, TT, D], F32R, A_H)
        hlo = at("hlo", [P, TT, D], F32R, A_H + 8192)
        A_XG = A_H + 16384
        xg = at("xg", [P, 2, GE, KD, 2, CAP], F32R, A_XG)
        hT = at("hT", [P, KD, T], F32, A_XG)
        A_HI = A_XG + 32768
        whi = at("whi", [P, 4, 2, 2 * FF], F32R, A_HI)
        wlo = at("wlo", [P, 4, 2, 2 * FF], F32R, A_HI + 16384)
        A_O = A_HI + 32768
        ohi = at("ohi", [P, D], F32R, A_O)
        olo = at("olo", [P, D], F32R, A_O + 4096)
        h = at("h", [P, TT, D], F32, A_O)
        A_S = A_O + 8192
        sel = at("sel", [P, TT, GS], F32R, A_S)
        selT = at("selT", [P, 2, 2, T], F32R, A_S + 2048)
        gain = at("gain", [P, D], F32, A_S)
        A_W = A_S + 2048 + 4096
        flo = at("flo", [64, 2 * FF], F32, A_W)
        gu = at("gu", [64, 2 * FF], F32, A_W + 2048)
        act = at("act", [64, FF], F32, A_W + 4096)
        actT = at("actT", [P, 2, CAP], F32, A_W + 5120)
        A_R = A_W + 5632
        RS = 6144
        assert A_R + 4 * RS * 4 <= 229368
        ring = [at(f"ring{s}", [P, RS], F32, A_R + s * RS * 4) for s in range(4)]
        PS = ctx.enter_context(nc.psum_tensor("PS", [P, 8, 512], F32))
        rpbr = nc.dram_tensor("rpbr", (NH * (2 * WR - 1), 2 * WC - 1), F32, kind="Internal").ap()
        ud = nc.dram_tensor("ud", (SW, T), F32, kind="Internal").ap()
        yd = nc.dram_tensor("yd", (SW, T), F32, kind="Internal").ap()

        def kp(w, k):
            return w.rearrange("(p k) n -> p k n", k=k)

        items = []

        def item(s, *parts):
            items.append((s, parts))
            return len(items) - 1

        IT = {}
        IT["w_in"] = item(0, (0, kp(I["s5_w_in"][0], KD)))
        wo_s5 = I["s5_w_out"][0].rearrange("(k p) n -> p k n", p=P)
        IT["w_out"] = [item(0, (0, wo_s5[:, :, 0:D])), item(1, (0, wo_s5[:, :, D:2 * D]))]
        moe_item = []
        off_moe = []

        def moe_items(i, s0):
            off_moe.append(s0)
            moe_item.append(len(items))
            for e in range(NE):
                g, j = divmod(e, EG)
                item((e + s0) % 4,
                     (0, I["moe_w_gate"][i, g, j].rearrange("(p k) n -> p (k n)", k=KD)),
                     (2048, I["moe_w_up"][i, g, j].rearrange("(p k) n -> p (k n)", k=KD)),
                     (4096, I["moe_w_down"][i, g, j].rearrange("(p k) n -> p (k n)", k=2)))

        def ple_items(i, s0):
            wg = kp(I["ple_w_gate"][i], KD)
            a = item(s0 % 4, (0, wg[:, :, 0:512]))
            b = item((s0 + 1) % 4, (0, I["ple_w_proj"][i].rearrange("(p k) n -> p (k n)", k=2)),
                     (2048, I["p"][i, 0, 0:P, :]), (2048 + 256, I["p"][i, 0, P:T, :]))
            c = item((s0 + 2) % 4, (0, wg[:, :, 512:1024]))
            return (a, b, c)

        moe_items(0, 2)
        IT["ple"] = [ple_items(0, 2)]
        wq = kp(I["nat_w_qkv"][0], KD)
        IT["qkv"] = [item((1 + n) % 4, (0, wq[:, :, 512 * n:512 * n + 512])) for n in range(6)]
        wo = I["nat_w_o"][0].rearrange("(k p) n -> p k n", p=P)
        IT["wo"] = [item((3 + n) % 4, (0, wo[:, :, 512 * n:512 * n + 512])) for n in range(2)]
        moe_items(1, 1)
        IT["ple"].append(ple_items(1, 1))
        prev, nth, last, cnt = [], [], {}, {}
        for n, (s, _) in enumerate(items):
            prev.append(last.get(s))
            last[s] = n
            cnt[s] = cnt.get(s, 0) + 1
            nth.append(cnt[s])

        done = {IT["w_in"]: ("u_done", 1)}
        done.update({n: ("glu_done", 4) for n in IT["w_out"]})
        for i in range(2):
            done.update({moe_item[i] + e: ("d_done", NE * i + e + 1) for e in range(NE)})
            done.update({n: ("ple_done", 4 * i + (2 if n == IT["ple"][i][0] else 4)) for n in IT["ple"][i]})
        done.update({n: ("qkv_done", 2 * w + 2) for w, n in enumerate(IT["qkv"])})
        done.update({n: ("wo_done", 2 * c + 2) for c, n in enumerate(IT["wo"])})
        loaded = [S(f"slot_loaded{s}") for s in range(4)]

        def arrived(eng, n):
            eng.wait_ge(loaded[items[n][0]], 48 * nth[n])

        def expert_loaded(i, g, jj):
            return (g + (nth[moe_item[i] + jj % GE] + jj // GE)) * 48

        UNITS = [(["selT", 0], [1, 2]), ([3], [4, 5]), (["wslot", 6], [7]), ([], [])]
        ALL_UNITS = ["selT", "wslot", 0, 1, 2, 3, 4, 5, 6, 7]
        M_POS, m_ = [], 0
        for a_, b_ in UNITS:
            M_POS.append((m_, m_ + 1, m_ + 1 + len(a_)))
            m_ += 1 + len(a_) + len(b_)
        assert m_ == 14
        M_BASE = len(ALL_UNITS) + m_ * (NSTEP - 1) + GE
        NSTEP_SEL = NSTEP + 1

        def WSLOT_M(i, g, jj):
            if isinstance(g, int) and g * GE + jj < GE:
                return M_BASE * i + 2
            at_ = M_POS[2][1] + 1
            return M_BASE * i + 10 + 14 * (g + (jj // GE - 1)) + at_

        block = ctx.enter_context(nc.Block())

        gains = [I["norm_mix"][0], I["norm_ffn"][0], I["norm_ple"][0],
                 I["norm_mix"][1], I["norm_ffn"][1], I["norm_ple"][1]]

        O1 = A_R + RS * 4
        s5W = at("s5W", [P, 2, SG, L, SH], F32, A_XG)
        s5V = at("s5V", [P, 2, SG, L, SH], F32, A_HI)
        s5WT = at("s5WT", [P, 2, SG, P], F32, A_R + 2 * RS * 4)
        s5T = at("s5T", [P, SG, P], F32, A_R + 2 * RS * 4 + 32768)
        ct = [at(f"ct{n}", [P, SG, NC_], F32, A_O + 4096 * n) for n in range(2)]
        s5hT = at("s5hT", [P, KD, T], F32, A_H)
        uT = at("uT", [P, SW // P, L, NC_], F32, A_H)
        us = at("us", [P, SG, NC_], F32, A_H + 4096)
        ct0, ct1 = ct
        tmpD = at("tmpD", [P, SG // 2, L, SH], F32, A_R + 2 * RS * 4 + 32768)
        tmpP = at("tmpP", [P, SG // 2, L, SH], F32, A_R + 2 * RS * 4 + 40960)
        tmsk = at("tmsk", [P, 2, 4, P], F32, A_S)
        braw = at("braw", [P, 2, SG, SH], F32, A_H + 8192)
        bbar = at("bbar", [P, 2, SG, SH], F32, A_H + 8192 + 4096)
        stab = at("stab", [P, SG, NC_], F32, A_H + 8192)
        ctab = at("ctab", [P, SG, NC_], F32, A_W)
        rp = at("rp", [NH * (2 * WR - 1) // 2, 2, 2 * WC - 1], F32, A_W + 4096)
        rpf = at("rpf", [NH * (2 * WR - 1) // 2, 2, 2 * WC - 1], F32, A_W + 4352)
        dec = at("dec", [P, SG, NC_], F32, O1 + 18432)
        craw = at("craw", [P, 2, 4, 2, SP_], F32, A_R + 16384)
        cT = at("cT", [P, 2, SG, SH], F32, A_R + 16384 + 4096)
        mask = at("mask", [P, 2, P], F32, A_S + 4096)
        lam = at("lam", [SG, 2, 2, SP_], F32, O1)
        ldt = at("ldt", [SG, 2], F32, O1 + 1024)
        dtt = at("dtt", [SG, 2], F32, O1 + 1056)
        pq = at("pq", [SG, 14, 2 * SP_], F32, O1 + 1088)
        prmT = at("prmT", [P, 4, SG], F32, O1 + 8256)
        wp_i = at("wp_i", [P, L], I32, O1 + 8768)
        wp = at("wp", [P, L], F32, O1 + 8800)
        cidx_i = at("cidx_i", [P, NC_], I32, O1 + 8832)
        cidx = at("cidx", [P, NC_], F32, O1 + 8960)
        t32 = at("t32", [P, 4, SG], F32, O1 + 9088)
        pw = at("pw", [P, 8, SG, L], F32, O1 + 9600)
        sc = [at(f"sc{n}", [P, SG, NC_], F32, A_XG + 4096 * n) for n in range(8)]
        yT = [at(f"yT{n}", [P, SW // P, T], F32, A_XG + 4096 * n) for n in range(5)]
        glu = [at(f"glu{n}", [P, 512], F32, A_XG + 20480 + 2048 * n) for n in range(2)]

        RX = A_XG + 16384
        wr = at("wr", [P, KD, NG + NE], F32, RX)
        rbias = at("rbias", [P, NG + NE], F32, RX + 1152)
        gl = at("gl", [P, TT, 8], F32, RX + 1312)
        el = at("el", [P, TT, NE], F32, RX + 1376)
        gmx = at("gmx", [P, TT, 8], F32, RX + 1632)
        gix = at("gix", [P, TT, 8], U32, RX + 1696)
        gf = at("gf", [P, TT], F32, RX + 1760)
        oh = at("oh", [P, TT, NG], F32, RX + 1792)
        eo = at("eo", [P, TT, NE], F32, RX + 1824)
        ch = at("ch", [P, TT, EG], F32, RX + 2080)
        emx = at("emx", [P, TT, 8], F32, RX + 2144)
        eix = at("eix", [P, TT, 8], U32, RX + 2208)
        ef = at("ef", [P, 2, TT], F32, RX + 2272)
        eid = at("eid", [P, 2, TT], F32, RX + 2304)
        gex = at("gex", [P, TT, NG], F32, RX + 2336)
        gsum = at("gsum", [P, TT], F32, RX + 2368)
        dlt = at("dlt", [P, TT], F32, RX + 2400)
        e21 = at("e21", [P, TT], F32, RX + 2432)
        wgt = at("wgt", [P, 2, TT], F32, RX + 2464)
        ngm = at("ngm", [P, TT], F32, RX + 2496)
        eq = at("eq", [P, 2, TT, NE], F32, RX + 2528)
        msk = at("msk", [P, TT, NE], F32, RX + 3040)
        pos = at("pos", [P, TT, NE], F32, RX + 3296)
        ptmp = at("ptmp", [P, 2, TT, NE], F32, RX + 3552)
        pch = at("pch", [P, 2, TT], F32, RX + 4064)
        val = at("val", [P, 2, TT], F32, RX + 4096)
        v2 = at("v2", [P, 2, TT], F32, RX + 4128)
        den = at("den", [P, TT], F32, RX + 4160)

        qk = at("qk", [P, TT, 2 * NH, HD], F32, A_HI)
        vt = at("vt", [P, TT, D], F32, A_HI + 16384)
        sq = at("sq", [P, 2 * NH, HD], F32, A_HI + 24576)
        qss = at("qss", [P, TT, 2 * NH], F32, A_W)
        qms = at("qms", [P, TT, 2 * NH], F32, A_W + 256)
        qrs = at("qrs", [P, TT, 2 * NH], F32, A_W + 512)
        qkw = at("qkw", [P, 2], F32, A_W + 1024)
        qT = at("qT", [P, NH // 2, T], F32, A_XG + 16384)
        kT = at("kT", [P, NH // 2, T], F32, A_XG + 24576)
        oT = at("oT", [P, NH // 2, T], F32, A_O)
        bias = [at("bias_a", [P, NH // 2, TT, ROWS, GW], F32, A_H),
                at("bias_b", [P, NH // 2, TT, ROWS, GW], F32, A_HI)]
        prob = at("prob", [P, 2, TT, T], F32, A_XG)
        probT = at("probT", [P, 2, 2, T], F32, A_XG + 4096)
        qkw8 = at("qkw8", [P, 1], F32, A_W + 1152)
        mx = at("mx", [P, 2, TT], F32, A_W + 1056)
        rs = at("rs", [P, 2, TT], F32, A_W + 1088)
        rr = at("rr", [P, 2, TT], F32, A_W + 1120)
        pT = at("pT", [P, 2, T], F32, A_H)
        sg = [at(f"sg{n}", [P, 512], F32, A_H + 2048 + 2048 * n) for n in range(2)]
        pr = [at(f"pr{n}", [P, 512], F32, A_H + 6144 + 2048 * n) for n in range(2)]

        oh_ov = at("oh_ov", [P, TT, CAP], F32, A_S)
        xo = at("xo", [P, KD, CAP], F32, A_XG)
        selTo = at("selTo", [CAP, T], F32, A_XG + 2048)
        oo = at("oo", [CAP, D], F32, A_XG + 4096)
        slu = at("slu", [CAP, FF], F32, A_XG + 8192)
        wso = at("wso", [CAP, 1], F32, A_XG + 9216)
        acto = at("acto", [CAP, FF], F32, A_XG + 9248)
        actTo = at("actTo", [P, 2, CAP], F32, A_XG + 10272)
        pr1 = at("pr1", [P, 2, TT], F32, RX + 4192)
        past = at("past", [P, 1], F32, RX + 4224)
        NOV = 3 * NE

        def overflow(eng, i, body, first=None, last=None):
            eng.wait_ge(S("many_ready"), i + 1)
            with eng.If(eng.value_load(many[0:1, 0:1], min_val=0, max_val=2 * T) > 0):
                if first:
                    first()
                with eng.Fori(0, NOV) as n:
                    body(n)
                if last:
                    last()

        def seq(eng, sem):
            n = [0]

            def link(ins):
                n[0] += 1
                ins.then_inc(sem, 1)
                eng.wait_ge(sem, n[0])
            return link

        NB = 4

        @block.sync
        def _(sp):
            def load(n):
                s, parts = items[n]
                if prev[n] is not None:
                    name, value = done[prev[n]]
                    sp.wait_ge(S(name), value)
                for j, (c, src) in enumerate(parts):
                    w = 1
                    for m in src.shape[1:]:
                        w *= m
                    dst = ring[s][:, c:c + w]
                    if len(src.shape) == 3:
                        dst = dst.rearrange("p (k n) -> p k n", k=src.shape[1])
                    sp.dma_start(dst, src).then_inc(loaded[s], 48 - 16 * (len(parts) - 1) if j == 0 else 16)

            sp.dma_start(x[:, :, :], I["x"][0].rearrange("(a p) d -> p a d", p=P)).then_inc(S("x_loaded"), 16)
            load(IT["w_in"])
            sp.wait_ge(S("uT_half"), 2)
            sp.dma_start(ud.rearrange("(k p) t -> p k t", p=P),
                         uT[:, :, :, :].rearrange("p k s c -> p k (s c)")).then_inc(S("ud_written"), 16)
            sp.wait_ge(S("ud_written"), 16)
            uv = ud.rearrange("(g h) (s c) -> s h g c", h=SH, s=L)
            for s in range(L):
                sp.dma_start(us[SH * s:SH * s + SH, :, :], uv[s]).then_inc(S("us_loaded"), 16)
            load(IT["w_out"][0])
            sp.wait_ge(S("dec_ready"), 1)
            sp.wait_ge(S("s5V_re"), 2)
            load(IT["w_out"][1])
            yv = yd.rearrange("(g h) (s c) -> s h g c", h=SH, s=L)
            sp.wait_ge(S("ys_half"), 2)
            for s in range(L):
                sp.dma_start(yv[s], sc[6][SH * s:SH * s + SH, :, :]).then_inc(S("yd_written"), 16)
            sp.wait_ge(S("yd_written"), 16 * L)
            sp.dma_start(yT[0][:, :, :], yd.rearrange("(k p) t -> p k t", p=P)).then_inc(S("yT_loaded"), 16)
            for i in range(2):
                m0 = moe_item[i]
                for e in range(GE):
                    load(m0 + e)
                wviews = [I["moe_w_gate"][i].rearrange("g j (p k) n -> p (g j) (k n)", k=KD),
                          I["moe_w_up"][i].rearrange("g j (p k) n -> p (g j) (k n)", k=KD),
                          I["moe_w_down"][i].rearrange("g j (p k) n -> p (g j) (k n)", k=2)]
                with sp.Fori(1, NSTEP) as g:
                    for j in range(GE):
                        s = items[m0 + j][0]
                        sp.wait_ge(S("d_done"), g * GE + (NE * i + j - GE + 1))
                        for c, w in enumerate(wviews):
                            sp.dma_start(ring[s][:, 2048 * c:2048 * c + 2048],
                                         w[:, bass.ds(g * GE + j, 1), :].rearrange("p e n -> p (e n)"))\
                                .then_inc(loaded[s], 16)
                def more(n):
                    sp.wait_ge(S(f"ov_free{i}"), n + 1)
                    e = n % NE
                    for c, w in enumerate(wviews):
                        sp.dma_start(ring[s_ov][:, 2048 * c:2048 * c + 2048],
                                     w[:, bass.ds(e, 1), :].rearrange("p e n -> p (e n)"))\
                            .then_inc(S(f"ov_loaded{i}"), 16)

                s_ov = items[m0][0]
                sp.wait_ge(S("d_done"), NE * (i + 1))
                overflow(sp, i, more, lambda: sp.sem_inc(S(f"ov_free{i}"), 1),
                         lambda: sp.wait_ge(S(f"ov_free{i}"), NOV + 1))
                for n in IT["ple"][i]:
                    load(n)
                if i == 0:
                    for n in IT["qkv"] + IT["wo"]:
                        load(n)
            sp.wait_ge(S("x_out"), 1)
            sp.dma_start(out[0].rearrange("(a p) d -> p a d", p=P), x[:, :, :]).then_inc(S("stored"), 16)
            sp.wait_ge(S("stored"), 16)

        @block.gpsimd
        def _(pool):
            link = seq(pool, S("pool_own"))
            pool.memset(ident[:, :], 0.0)
            pool.memset(mask[:, :, :], 1.0)
            pool.memset(tri[:, :], 1.0)
            pool.memset(ones[:, :], 1.0)
            pool.memset(mhalf[:, :], -0.5)
            link(pool.memset(negh[:, :], 0.0))
            pool.affine_select(out=ident[:, :], in_=ident[:, :], compare_op=ALU.not_equal, fill=1.0, base=0,
                               pattern=[[-1, P]], channel_multiplier=1).then_inc(S("ident_ready"), 1)
            pool.affine_select(out=tri[:, :], in_=tri[:, :], compare_op=ALU.is_gt, fill=0.0, base=0,
                               pattern=[[1, P]], channel_multiplier=-1)
            pool.affine_select(out=mask[:, 0, :], in_=mask[:, 0, :], compare_op=ALU.is_ge, fill=0.0,
                               base=SH - 1, pattern=[[SH, L], [0, SH]], channel_multiplier=-1)
            link(pool.affine_select(out=mask[:, 1, :], in_=mask[:, 1, :], compare_op=ALU.is_ge, fill=0.0,
                                    base=0, pattern=[[-SH, L], [0, SH]], channel_multiplier=1))
            link(pool.iota(wp_i[0:64, :], pattern=[[-1, L]], base=L - 1, channel_multiplier=0))
            link(pool.iota(wp_i[64:P, :], pattern=[[1, L]], base=0, channel_multiplier=0))
            link(pool.iota(cidx_i[0:64, :], pattern=[[1, NC_]], base=0, channel_multiplier=0))
            link(pool.iota(cidx_i[64:P, :], pattern=[[-1, NC_]], base=NC_ - 1, channel_multiplier=0))
            link(pool.iota(iota_i[:, :], pattern=[[1, GS]], base=0, channel_multiplier=0))
            pool.tensor_copy(wp[:, :], wp_i[:, :])
            pool.tensor_copy(cidx[:, :], cidx_i[:, :])
            pool.tensor_copy(iota_slot[:, :], iota_i[:, :])
            pool.tensor_copy(iota_e[:, :], iota_i[:, 0:NE])
            for b in (0, 64):
                link(pool.affine_select(out=negh[b:b + 64, 0:GW - WC], in_=negh[b:b + 64, 0:GW - WC],
                                        compare_op=ALU.is_ge, fill=MASKV, base=WC // 2,
                                        pattern=[[1, GW - WC]], channel_multiplier=-1))
                link(pool.affine_select(out=negh[b:b + 64, WC:GW], in_=negh[b:b + 64, WC:GW],
                                        compare_op=ALU.is_ge, fill=MASKV, base=WC // 2 - 1 - WC,
                                        pattern=[[-1, GW - WC]], channel_multiplier=1))
            pool.tensor_copy(mhalf[:, :], mhalf[:, :]).then_inc(S("consts"), 1)

            def norm_pow(n):
                pool.wait_ge(S("ms_ready"), n + 1)
                pool.tensor_tensor(rstd[:, 0:TT], ms[:, 0:TT], mhalf[:, 0:TT], ALU.pow).then_inc(S("rstd_ready"), 1)

            pool.dma_start(rp[:, :, :], I["nat_rpb"][0].rearrange("a b c -> (a b) c").rearrange("(p a) c -> p a c", a=2))\
                .then_inc(S("rp_loaded"), 16)
            pool.wait_ge(S("rp_loaded"), 16)
            link(pool.tensor_copy(rpf[:, :, :], rp[:, :, ::-1]))
            pool.dma_start(rpbr.rearrange("(p a) c -> p a c", a=2), rpf[:, :, :]).then_inc(S("rpbr_written"), 16)

            norm_pow(0)
            pool.wait_ge(S("cT_ready"), 2)
            pool.wait_ge(S("pw_ready"), 1)
            for q in range(2):
                g0 = slice(16 * q, 16 * q + 16)
                link(pool.tensor_tensor(s5V[:, 0, g0], bc(cT[:, 0, g0], 2, L), bc(pw[:, 2, g0], 3, SH), ALU.mult))
                link(pool.tensor_tensor(tmpP[:, :, :, :], bc(cT[:, 1, g0], 2, L), bc(pw[:, 7, g0], 3, SH), ALU.mult))
                pool.tensor_tensor(s5V[:, 0, g0], s5V[:, 0, g0], tmpP[:, :, :, :], ALU.add)\
                    .then_inc(S("s5V_re"), 1)
                pool.wait_ge(S("s5V_re"), q + 1)
            pool.wait_ge(S("rpbr_written"), 16)
            norm_pow(1)
            norm_pow(2)
            norm_pow(3)
            for part in range(2):
                if part == 0:
                    pool.wait_ge(S("x_ready"), 3)
                else:
                    pool.wait_ge(S("k_T"), 2 * TT)
                hp = NH // 2
                for rq in range(ROWS):
                    for rk in range(ROWS):
                        off = part * hp * (2 * WR - 1) * (2 * WC - 1) + (rk - rq + WR - 1) * (2 * WC - 1) + WC - GW
                        src = bass.AP(rpbr.tensor, off,
                                      [[1, GW], [(2 * WR - 1) * (2 * WC - 1), hp], [1, GW]])
                        p0 = 64 * (rq % 2)
                        pool.dma_start(bias[part][p0:p0 + 64, :, rq // 2, rk, :], src)\
                            .then_inc(S(f"bias_loaded{part}"), 16)
                pool.wait_ge(S(f"bias_loaded{part}"), 16 * ROWS * ROWS)
                for hh in range(hp):
                    b = bias[part][:, hh].rearrange("p a r c -> p (a r) c")
                    pool.tensor_tensor(b, b, bc(negh[:, ::-1], 1, TT * ROWS), ALU.add).then_inc(S("bias_ready"), 1)
                if part == 0:
                    for t in range(TT):
                        pool.wait_ge(S("qms_ready"), t + 1)
                        pool.tensor_tensor(qrs[:, t, :], qms[:, t, :], mhalf[:, :], ALU.pow)\
                            .then_inc(S("qrs_ready"), 1)
            norm_pow(4)
            norm_pow(5)

        @block.scalar
        def _(ac):
            link = seq(ac, S("act_own"))
            ac.dma_start(lam[:, 0], I["s5_lam_re"][0].rearrange("d g p -> g d p")).then_inc(S("lam_loaded"), 16)
            ac.dma_start(lam[:, 1], I["s5_lam_im"][0].rearrange("d g p -> g d p")).then_inc(S("lam_loaded"), 16)
            ac.dma_start(ldt[:, :], I["s5_log_dt"][0].rearrange("d g -> g d"), allow_slow_non_contiguous=True).then_inc(S("lam_loaded"), 16)
            for c, nm in enumerate(("s5_c_re", "s5_c_im")):
                for d in range(2):
                    ac.dma_start(craw[:, c, :, d, :], I[nm][0, d].rearrange("(a b) h p -> (b h) a p", b=8))\
                        .then_inc(S("c_loaded"), 16)
            for c, nm in enumerate(("s5_b_re", "s5_b_im")):
                for d in range(2):
                    ac.dma_start(braw[64 * d:64 * d + 64, c], I[nm][0, d].rearrange("g p h -> p g h"))\
                        .then_inc(S("b_loaded"), 16)
            ac.dma_start(dskip[:, :], I["s5_d"][0].rearrange("(k p) -> p k", p=P), allow_slow_non_contiguous=True).then_inc(S("d_loaded"), 16)

            def norm_sq(n, moe=None):
                if n == 0:
                    ac.wait_ge(S("x_loaded"), 16)
                else:
                    ac.wait_ge(S("x_ready"), n)
                ac.dma_start(gain[:, :], bc(gains[n], 0, P)).then_inc(S("gain_loaded"), 16)
                if moe is not None:
                    ac.dma_start(wr[:, :, 0:NG], kp(I["moe_w_group"][moe], KD)).then_inc(S("router_loaded"), 16)
                    ac.dma_start(wr[:, :, NG:], kp(I["moe_w_expert"][moe], KD)).then_inc(S("router_loaded"), 16)
                    ac.dma_start(rbias[:, 0:NG], bc(I["moe_b_group"][moe], 0, P)).then_inc(S("router_loaded"), 16)
                    ac.dma_start(rbias[:, NG:], bc(I["moe_b_expert"][moe], 0, P)).then_inc(S("router_loaded"), 16)
                for t in range(TT):
                    ac.activation(h[:, t, :], x[:, t, :], ACT.Square, accum_out=ss[:, t:t + 1])\
                        .then_inc(S("ss_ready"), 1)

            def norm_evict(n, dst):
                for kq in range(2):
                    ac.wait_ge(S("h_T"), 2 * n + kq + 1)
                    ac.activation(dst[:, 4 * kq:4 * kq + 4, 0:P], PS[:, NB + kq, :].rearrange("p (k t) -> p k t", k=4),
                                  ACT.Copy).then_inc(S("hT_a"), 1)

            ac.wait_ge(S("lam_loaded"), 48)
            ac.activation(dtt[:, :], ldt[:, :], ACT.Exp).then_inc(S("dt_ready"), 1)
            ac.wait_ge(S("ang_ready"), 1)
            ac.activation(pq[:, 5], pq[:, 0], ACT.Exp).then_inc(S("trig_ready"), 1)
            ac.activation(pq[:, 6], pq[:, 3], ACT.Sin).then_inc(S("trig_ready"), 1)
            ac.activation(pq[:, 7], pq[:, 4], ACT.Sin).then_inc(S("trig_ready"), 1)
            for c in range(2):
                ac.wait_ge(S("c_T"), c + 1)
                ac.activation(cT[:, c], PS[:, 1 + c, :].rearrange("p (g h) -> p g h", h=SH), ACT.Copy)\
                    .then_inc(S("cT_ready"), 1)
            ac.wait_ge(S("phase_ready"), 1)
            ac.activation(pw[:, 3], pw[:, 0], ACT.Exp)
            ac.activation(pw[:, 4], pw[:, 0], ACT.Exp, scale=-1.0)
            ac.activation(t32[:, 1], prmT[:, 0], ACT.Exp, scale=float(L))
            ac.activation(pw[:, 5], pw[:, 1], ACT.Sin, scale=TURN)
            ac.activation(pw[:, 6], pw[:, 2], ACT.Sin, scale=TURN).then_inc(S("powx_ready"), 1)
            norm_sq(0)
            norm_evict(0, s5hT)
            ac.wait_ge(S("u_done"), 1)
            for b in range(2):
                ac.activation(uT[:, 2 * b:2 * b + 2].rearrange("p k s c -> p k s c"),
                              PS[:, 4 + b, :].rearrange("p (k c s) -> p k s c", k=2, s=L), ACT.Copy)\
                    .then_inc(S("uT_half"), 1)
            for n in range(SG // 2):
                ac.wait_ge(S("W_T"), n + 1)
                ac.activation(s5WT[:, :, 2 * n:2 * n + 2, :].rearrange("p r g n -> p g r n"),
                              PS[:, 2 + n % 2, :].rearrange("p (g r n) -> p g r n", g=2, r=2), ACT.Copy)\
                    .then_inc(S("WT_ready"), 1)
            ac.wait_ge(S("cphase_ready"), 1)
            ac.activation(stab[:, :, :], ct0[:, :, :], ACT.Sin, scale=TURN)
            ac.activation(ctab[:, :, :], ct1[:, :, :], ACT.Sin, scale=TURN).then_inc(S("ctab_ready"), 1)
            ac.wait_ge(S("y_done"), 1)
            for b in range(2):
                ac.activation(sc[6][:, 16 * b:16 * b + 16, :], PS[:, 2 + b, :].rearrange("p (g c) -> p g c", c=NC_),
                              ACT.Copy).then_inc(S("ys_half"), 1)
            ac.wait_ge(S("inner_ready"), 1)
            ac.activation(yT[3][:, :, :], yT[2][:, :, :], ACT.Tanh, scale=math.sqrt(2 / math.pi))\
                .then_inc(S("tanh_ready"), 1)
            for n in range(4):
                ac.wait_ge(S("glu_done"), n + 1)
                if n >= 2:
                    ac.wait_ge(S("glu_used"), n - 1)
                ac.activation(glu[n % 2][:, :], PS[:, 5 + 2 * (n % 2), :], ACT.Sigmoid).then_inc(S("sig_ready"), 1)

            def evict(m, dst, src):
                ac.wait_ge(S("m_written"), m + 1)
                ac.activation(dst, src, ACT.Copy).then_inc(S("m_evicted"), 1)

            def chunk(i, g, jj, c):
                n = 4 * NE * i + 4 * GE * g + 4 * jj + c
                s = items[moe_item[i] + jj % GE][0]
                if c == 0:
                    ac.wait_ge(loaded[s], expert_loaded(i, g, jj))
                if not (isinstance(n, int) and n < 4):
                    ac.wait_ge(S("split_used"), n - 3)
                r = ring[s][:, 0:4096].rearrange("p (u n) -> p u n", u=2)[:, :, 512 * c:512 * c + 512]
                ac.activation(whi[:, c].rearrange("p k (u f) -> p u k f", u=2),
                              r.rearrange("p u (k f) -> p u k f", k=2), ACT.Copy).then_inc(S("hi_ready"), 1)

            def fold(i, e):
                ac.wait_ge(S("gu_done"), NE * i + e + 1)
                ac.activation(flo[:, :], PS[64:P, 0, :], ACT.Copy).then_inc(S("flo_ready"), 1)

            def silu(i, e):
                ac.wait_ge(S("gu_ready"), NE * i + e + 1)
                ac.activation(act[:, :], gu[:, 0:FF], ACT.Silu).then_inc(S("silu_ready"), 1)

            def units(i, par, lst, m):
                for n, u in enumerate(lst):
                    if u == "selT":
                        evict(m + n, selT[:, par].rearrange("p a t -> p (a t)"), PS[:, 1, :])
                    elif u == "wslot":
                        evict(m + n, wslot[0:64, par, :], PS[0:64, 1, 0:GE])
                    else:
                        evict(m + n, xg[:, par, :, u].rearrange("p e c j -> p c e j"),
                              PS[:, 1, :].rearrange("p (c e j) -> p c e j", c=2, e=GE))

            def step(i, g, par, j, last):
                e = g * GE + j
                m = M_BASE * i + 10 + 14 * g
                evict(m + (j if last else M_POS[j][0]), actT[:, :, :].rearrange("p a t -> p (a t)"),
                      PS[:, 1, 0:2 * CAP])
                more = not (last and j >= 2)
                nxt = not (last and j == 3)
                if more:
                    chunk(i, g, j + 2, 0)
                    chunk(i, g, j + 2, 1)
                if nxt:
                    fold(i, e + 1)
                if not last:
                    units(i, 1 - par, UNITS[j][0], m + M_POS[j][1])
                if more:
                    chunk(i, g, j + 2, 2)
                if nxt:
                    silu(i, e + 1)
                if more:
                    chunk(i, g, j + 2, 3)
                if not last:
                    units(i, 1 - par, UNITS[j][1], m + M_POS[j][2])
                if j % 2:
                    pair = g * 2 + j // 2 + NE // 2 * i
                    ac.wait_ge(S("d_done"), NE * i + e + 1)
                    if not (isinstance(pair, int) and pair == 0):
                        ac.wait_ge(S("comb_done"), pair)
                    for n in range(2):
                        ac.activation(ohi[:, 512 * n:512 * n + 512], PS[:, 2 + n, :], ACT.Copy)\
                            .then_inc(S("ohi_ready"), 1)

            def moe(i):
                norm_sq(1 + 3 * i, moe=i)
                norm_evict(1 + 3 * i, hT)
                for c in range(2):
                    chunk(i, 0, 0, c)
                ac.wait_ge(S("top_ready"), i + 1)
                for t in range(TT):
                    ac.activation(gex[:, t, :], gl[:, t, 0:NG], ACT.Exp, bias=ngm[:, t:t + 1],
                                  accum_out=gsum[:, t:t + 1])
                ac.activation(e21[:, :], dlt[:, :], ACT.Exp).then_inc(S("gex_ready"), 1)
                for c in range(2, 4):
                    chunk(i, 0, 0, c)
                units(i, 0, ALL_UNITS, M_BASE * i)
                chunk(i, 0, 1, 0)
                chunk(i, 0, 1, 1)
                fold(i, 0)
                chunk(i, 0, 1, 2)
                silu(i, 0)
                chunk(i, 0, 1, 3)
                for j in range(GE):
                    step(i, 0, 0, j, False)
                with ac.Fori(0, (NSTEP - 2) // 2) as r:
                    for sub in (1, 2):
                        for j in range(GE):
                            step(i, r * 2 + sub, sub % 2, j, False)
                for j in range(GE):
                    step(i, NSTEP - 1, 1, j, True)
                moe_more(i)

            def moe_more(i):
                def more(n):
                    name = lambda what: S(f"ov_{what}{i}")
                    ac.wait_ge(name("gu"), n + 1)
                    ac.activation(slu[:, :], PS[0:CAP, 2, 0:FF], ACT.Silu).then_inc(name("silu"), 1)

                overflow(ac, i, more)

            def ple(i):
                norm_sq(2 + 3 * i)
                norm_evict(2 + 3 * i, hT)
                ac.wait_ge(S("p_T"), i + 1)
                ac.activation(pT[:, :, :].rearrange("p k t -> p (k t)"), PS[:, 0, :], ACT.Copy).then_inc(S("pT_ready"), 1)
                for n in range(4):
                    k = 4 * i + n
                    ac.wait_ge(S("ple_done"), k + 1)
                    if k >= 2:
                        ac.wait_ge(S("ple_used"), k - 1)
                    ac.activation(sg[n % 2][:, :], PS[:, 2 * (n % 2), :], ACT.Sigmoid).then_inc(S("sg_ready"), 1)

            moe(0)
            ple(0)

            norm_sq(3)
            for c, nm in enumerate(("nat_q_norm", "nat_k_norm")):
                for d in range(2):
                    ac.dma_start(qkw[64 * d:64 * d + 64, c:c + 1], I[nm][0].rearrange("(p a) -> p a", a=1))\
                        .then_inc(S("qkw_loaded"), 16)
            norm_evict(3, hT)
            for n in range(12):
                if n % 2 == 0:
                    ac.wait_ge(S("qkv_done"), n + 1)
                    w, t = n // 2, n % 2
                    dst = qk[:, 0, 8 * w:8 * w + 8, :].rearrange("p a d -> p (a d)") if w < 4 else \
                        vt[:, 0, 512 * (w - 4):512 * (w - 4) + 512]
                    ac.activation(dst, PS[:, n % 4, :], ACT.Copy).then_inc(S("qkv_a"), 1)
                if n == 6:
                    for t in range(TT):
                        ac.wait_ge(S("qkv_d"), 4)
                        ac.wait_ge(S("qkv_a"), 4)
                        if t:
                            ac.wait_ge(S("qss_ready"), t)
                        ac.activation(sq[:, :, :], qk[:, t], ACT.Square).then_inc(S("sq_ready"), 1)
            ac.wait_ge(S("qkw_loaded"), 64)
            link(ac.activation(qkw8[:, :], qkw[:, 0:1], ACT.Copy, scale=1 / math.sqrt(HD)))
            for t in range(TT):
                for n in range(2):
                    ac.wait_ge(S("q_T"), 2 * t + n + 1)
                    ac.activation(qT[:, 4 * n:4 * n + 4, P * t:P * t + P],
                                  PS[:, 4 + n, :].rearrange("p (a t) -> p a t", a=4), ACT.Copy,
                                  scale=qkw8[:, 0:1]).then_inc(S("qT_ready"), 1)
            for a in range(NH + 1):
                if a < NH:
                    ac.wait_ge(S("mx_ready"), a + 1)
                    for t in range(TT):
                        ac.activation(prob[:, a % 2, t, :], prob[:, a % 2, t, :], ACT.Exp, bias=mx[:, a % 2, t:t + 1],
                                      accum_out=rs[:, a % 2, t:t + 1]).then_inc(S("exp_ready"), 1)
                if a >= 1:
                    b = a - 1
                    ac.wait_ge(S("prob_T"), b + 1)
                    if b >= 2:
                        ac.wait_ge(S("pv_done"), b - 1)
                    ac.activation(probT[:, b % 2].rearrange("p a t -> p (a t)"), PS[:, 2 + b % 2, :], ACT.Copy)\
                        .then_inc(S("probT_ready"), 1)
            moe(1)
            ple(1)

        @block.vector
        def _(ve):
            link = seq(ve, S("dve_own"))
            tt = ve.tensor_tensor
            ts = ve.tensor_scalar
            stt = ve.scalar_tensor_tensor

            def norm_scale(n):
                ve.wait_ge(S("ss_ready"), TT * (n + 1))
                ts(ms[:, 0:TT], ss[:, 0:TT], 1.0 / D, EPS, ALU.mult, ALU.add).then_inc(S("ms_ready"), 1)
                ve.wait_ge(S("gain_loaded"), 16 * (n + 1))
                ve.wait_ge(S("rstd_ready"), n + 1)
                for t in range(TT):
                    stt(h[:, t, :], x[:, t, :], rstd[:, t:t + 1], gain[:, :], ALU.mult, ALU.mult)\
                        .then_inc(S("h_ready"), 1)

            def norm_evict(n, dst):
                for kq in range(2):
                    ve.wait_ge(S("h_T2"), 2 * n + kq + 1)
                    ve.tensor_copy(dst[:, 4 * kq:4 * kq + 4, P:T],
                                   PS[:, NB + 2 + kq, :].rearrange("p (k t) -> p k t", k=4)).then_inc(S("hT_d"), 1)

            ve.wait_ge(S("lam_loaded"), 48)
            ve.wait_ge(S("dt_ready"), 1)
            v = [pq[:, n].rearrange("g (d p) -> g d p", d=2) for n in range(14)]
            for d in range(2):
                ts(v[0][:, d], lam[:, 0, d, :], dtt[:, d:d + 1], None, ALU.mult)
                link(ts(v[1][:, d], lam[:, 1, d, :], dtt[:, d:d + 1], None, ALU.mult))
            link(ts(v[2], v[1], 1 / (2 * math.pi), MAGIC, ALU.mult, ALU.add))
            link(ts(v[2], v[2], MAGIC, None, ALU.subtract))
            link(stt(v[3], v[2], -TWO_PI_HI, v[1], ALU.mult, ALU.add))
            link(stt(v[3], v[2], -TWO_PI_LO, v[3], ALU.mult, ALU.add))
            link(ts(v[3], v[3], TURN / 2, -TURN / 2, ALU.min, ALU.max))
            link(stt(v[4], v[3], -1.0, v[3], ALU.mult, ALU.min))
            ts(v[4], v[4], math.pi / 2, None, ALU.add).then_inc(S("ang_ready"), 1)
            re, im = lam[:, 0], lam[:, 1]
            link(tt(v[10], re, re, ALU.mult))
            link(tt(v[11], im, im, ALU.mult))
            link(tt(v[10], v[10], v[11], ALU.add))
            link(ve.reciprocal(v[10], v[10]))
            ve.wait_ge(S("trig_ready"), 3)
            link(tt(v[8], v[5], v[7], ALU.mult))
            link(tt(v[9], v[5], v[6], ALU.mult))
            link(ts(v[8], v[8], -1.0, None, ALU.add))
            link(tt(v[11], v[8], re, ALU.mult))
            link(tt(v[12], v[9], im, ALU.mult))
            link(tt(v[11], v[11], v[12], ALU.add))
            link(tt(v[12], v[9], re, ALU.mult))
            link(tt(v[13], v[8], im, ALU.mult))
            link(tt(v[12], v[12], v[13], ALU.subtract))
            link(tt(v[11], v[11], v[10], ALU.mult))
            link(tt(v[12], v[12], v[10], ALU.mult))
            ts(v[2], v[3], 1 / (2 * math.pi), None, ALU.mult).then_inc(S("coef_ready"), 1)
            ve.wait_ge(S("prm_T"), 1)
            link(ve.tensor_copy(prmT[:, :, :].rearrange("p a g -> p (a g)"), PS[:, 0, 0:4 * SG]))
            ve.wait_ge(S("consts"), 1)
            link(tt(pw[:, 0], bc(prmT[:, 0, :], 2, L), bc(wp[:, :], 1, SG), ALU.mult))
            link(tt(pw[:, 1], bc(prmT[:, 1, :], 2, L), bc(wp[:, :], 1, SG), ALU.mult))

            def turns(ph, quarter):
                link(ts(quarter, ph, MAGIC, None, ALU.add))
                link(ts(quarter, quarter, MAGIC, None, ALU.subtract))
                link(tt(ph, ph, quarter, ALU.subtract))
                link(stt(quarter, ph, -1.0, ph, ALU.mult, ALU.min))
                return ts(quarter, quarter, 0.25, None, ALU.add)

            turns(pw[:, 1], pw[:, 2]).then_inc(S("phase_ready"), 1)
            ve.wait_ge(S("b_loaded"), 64)
            cr, ci = bc(prmT[:, 2, :], 2, SH), bc(prmT[:, 3, :], 2, SH)
            tmp = tmpD[:, 0:4].rearrange("p g l h -> p (g l) h")
            link(tt(bbar[:, 0], braw[:, 0], cr, ALU.mult))
            link(tt(tmp, braw[:, 1], ci, ALU.mult))
            link(tt(bbar[:, 0], bbar[:, 0], tmp, ALU.subtract))
            link(tt(bbar[:, 1], braw[:, 1], cr, ALU.mult))
            link(tt(tmp, braw[:, 0], ci, ALU.mult))
            link(tt(bbar[:, 1], bbar[:, 1], tmp, ALU.add))
            ve.wait_ge(S("powx_ready"), 1)
            link(tt(pw[:, 0], pw[:, 3], pw[:, 6], ALU.mult))
            link(tt(pw[:, 1], pw[:, 3], pw[:, 5], ALU.mult))
            link(tt(pw[:, 2], pw[:, 4], pw[:, 6], ALU.mult))
            tt(pw[:, 7], pw[:, 4], pw[:, 5], ALU.mult).then_inc(S("pw_ready"), 1)
            norm_scale(0)
            norm_evict(0, s5hT)
            ve.wait_ge(S("pw_ready"), 1)
            td = tmpD[:, :, :, :]
            for q in range(2):
                gg = slice(16 * q, 16 * q + 16)
                br, bi = bc(bbar[:, 0, gg], 2, L), bc(bbar[:, 1, gg], 2, L)
                pr_, pi = bc(pw[:, 0, gg], 3, SH), bc(pw[:, 1, gg], 3, SH)
                link(tt(s5W[:, 0, gg], br, pr_, ALU.mult))
                link(tt(td, bi, pi, ALU.mult))
                link(tt(s5W[:, 0, gg], s5W[:, 0, gg], td, ALU.subtract))
                link(tt(s5W[:, 1, gg], br, pi, ALU.mult))
                link(tt(td, bi, pr_, ALU.mult))
                tt(s5W[:, 1, gg], s5W[:, 1, gg], td, ALU.add).then_inc(S("s5W_half"), 1)
                ve.wait_ge(S("s5W_half"), q + 1)
            ve.wait_ge(S("cT_ready"), 2)
            for q in range(2):
                gg = slice(16 * q, 16 * q + 16)
                link(tt(s5V[:, 1, gg], bc(cT[:, 0, gg], 2, L), bc(pw[:, 7, gg], 3, SH), ALU.mult))
                link(tt(td, bc(cT[:, 1, gg], 2, L), bc(pw[:, 2, gg], 3, SH), ALU.mult))
                tt(s5V[:, 1, gg], s5V[:, 1, gg], td, ALU.subtract).then_inc(S("s5V_im"), 1)
                ve.wait_ge(S("s5V_im"), q + 1)
            t8, t8n = t32[:, 2], t32[:, 3]
            link(ts(t8, prmT[:, 1, :], float(L), None, ALU.mult))
            link(ts(t8n, t8, MAGIC, None, ALU.add))
            link(ts(t8n, t8n, MAGIC, None, ALU.subtract))
            link(tt(t8, t8, t8n, ALU.subtract))
            link(tt(ct0[:, :, :], bc(t8, 2, NC_), bc(cidx[:, :], 1, SG), ALU.mult))
            turns(ct0[:, :, :], ct1[:, :, :]).then_inc(S("cphase_ready"), 1)
            link(ve.tensor_copy(dec[:, :, :], bc(t32[:, 1], 2, NC_)))
            ve.memset(dec[0:64, :, NC_ - 1:NC_], 0.0)
            ve.memset(dec[64:P, :, 0:1], 0.0).then_inc(S("dec_ready"), 1)
            ve.wait_ge(S("dec_ready"), 1)
            for n in range(SG // 4):
                ve.wait_ge(S("T_done"), 2 * n + 2)
                for d in range(2):
                    dn = tt(tmsk[:, d], PS[:, 2 * (n % 2) + d, :].rearrange("p (g n) -> p g n", g=4),
                            bc(mask[:, d, :], 1, 4), ALU.mult)
                link(dn)
                tt(s5T[:, 4 * n:4 * n + 4, :], tmsk[:, 0], tmsk[:, 1], ALU.add).then_inc(S("s5T_ready"), 1)
                ve.wait_ge(S("s5T_ready"), n + 1)
            ve.wait_ge(S("ctab_ready"), 1)
            ve.wait_ge(S("v_done"), 1)
            vr = PS[:, 4:6, :].rearrange("p b (g c) -> p (b g) c", c=NC_)
            vi = PS[:, 6:8, :].rearrange("p b (g c) -> p (b g) c", c=NC_)
            C_, S_ = ctab[:, :, :], stab[:, :, :]
            mr, mi, qr, qi, sr, si, ta, tb = [sc[n][:, :, :] for n in range(8)]
            link(tt(mr, vr, C_, ALU.mult))
            link(tt(ta, vi, S_, ALU.mult))
            link(tt(mi, vi, C_, ALU.mult))
            link(tt(tb, vr, S_, ALU.mult))
            link(tt(mr, mr, ta, ALU.add))
            link(tt(mi, mi, tb, ALU.subtract))
            N = SG * NC_
            fl = [sc[n][:, :, :].rearrange("p g c -> p (g c)") for n in range(4)]
            df = dec[:, :, :].rearrange("p g c -> p (g c)")
            for q in (2, 3):
                ve.memset(fl[q][0:64, 0:1], 0.0)
                link(ve.memset(fl[q][64:P, N - 1:N], 0.0))
            for m, q in ((0, 2), (1, 3)):
                link(ve.tensor_tensor_scan(fl[q][0:64, 1:N], fl[m][0:64, 0:N - 1], df[0:64, 0:N - 1], 0.0,
                                           ALU.add, ALU.mult))
                link(ve.tensor_tensor_scan(fl[q][64:P, N - 2::-1], fl[m][64:P, N - 1:0:-1], df[64:P, N - 1:0:-1],
                                           0.0, ALU.add, ALU.mult))
            link(tt(sr, qr, C_, ALU.mult))
            link(tt(ta, qi, S_, ALU.mult))
            link(tt(si, qr, S_, ALU.mult))
            link(tt(tb, qi, C_, ALU.mult))
            tt(sr, sr, ta, ALU.subtract).then_inc(S("S_ready"), 1)
            tt(si, si, tb, ALU.add).then_inc(S("S_ready"), 1)
            ve.wait_ge(S("yT_loaded"), 16)
            ve.wait_ge(S("d_loaded"), 16)
            uf = uT[:, :, :, :].rearrange("p k s c -> p k (s c)")
            for k in range(4):
                link(stt(yT[1][:, k, :], uf[:, k, :], dskip[:, k:k + 1], yT[0][:, k, :], ALU.mult, ALU.add))
            y1, y2, y3, y4 = [yT[n][:, :, :] for n in (1, 2, 3, 4)]
            link(tt(y2, y1, y1, ALU.mult))
            link(ts(y2, y2, 0.044715, 1.0, ALU.mult, ALU.add))
            tt(y2, y2, y1, ALU.mult).then_inc(S("inner_ready"), 1)
            ve.wait_ge(S("tanh_ready"), 1)
            link(ts(y3, y3, 0.5, 0.5, ALU.mult, ALU.add))
            sc_ = [y.rearrange("p k (s c) -> p k s c", s=L) for y in (y3, y1)]
            tt(y4.rearrange("p k (c s) -> p k s c", s=L), sc_[0], sc_[1], ALU.mult).then_inc(S("gelu_ready"), 1)
            for n in range(4):
                t, c = divmod(n, 2)
                ve.wait_ge(S("sig_ready"), n + 1)
                link(tt(glu[n % 2][:, :], PS[:, 4 + 2 * (n % 2), :], glu[n % 2][:, :], ALU.mult))
                xs = x[:, t, 512 * c:512 * c + 512]
                ins = tt(xs, xs, glu[n % 2][:, :], ALU.add)
                ins.then_inc(S("glu_used"), 1)
                ve.wait_ge(S("glu_used"), n + 1)
            ve.sem_inc(S("x_ready"), 1)

            def route(i):
                ve.memset(gl[:, :, :], 3 * MASKV)
                ve.wait_ge(S("router_loaded"), 64 * (i + 1))
                ve.wait_ge(S("logits_done"), i + 1)
                lp = PS[:, 0, 0:TT * (NG + NE)].rearrange("p (t n) -> p t n", t=TT)
                link(tt(el[:, :, :], lp[:, :, NG:], bc(rbias[:, NG:], 1, TT), ALU.add))
                link(tt(gl[:, :, 0:NG], lp[:, :, 0:NG], bc(rbias[:, 0:NG], 1, TT), ALU.add))
                for t in range(TT):
                    link(ve.max(gmx[:, t, :], gl[:, t, :]))
                    link(ve.max_index(gix[:, t, :], gmx[:, t, :], gl[:, t, :]))
                link(ve.tensor_copy(gf[:, :], gix[:, :, 0]))
                for t in range(TT):
                    link(ts(oh[:, t, :], iota_e[:, 0:NG], gf[:, t:t + 1], None, ALU.is_equal))
                link(tt(eo[:, :, :].rearrange("p t (g e) -> p t g e", g=NG),
                        el[:, :, :].rearrange("p t (g e) -> p t g e", g=NG), bc(oh[:, :, :], 3, EG), ALU.mult))
                for t in range(TT):
                    link(ve.tensor_reduce(ch[:, t, :], eo[:, t, :].rearrange("p (g e) -> p e g", g=NG), AX.X, ALU.add))
                for t in range(TT):
                    link(ve.max(emx[:, t, :], ch[:, t, :]))
                    link(ve.max_index(eix[:, t, :], emx[:, t, :], ch[:, t, :]))
                for j in range(2):
                    link(ve.tensor_copy(ef[:, j, :], eix[:, :, j]))
                    link(stt(eid[:, j, :], gf[:, :], float(EG), ef[:, j, :], ALU.mult, ALU.add))
                link(ts(ngm[:, :], gmx[:, :, 0], -1.0, None, ALU.mult))
                tt(dlt[:, :], emx[:, :, 1], emx[:, :, 0], ALU.subtract).then_inc(S("top_ready"), 1)
                for j in range(2):
                    for t in range(TT):
                        link(ts(eq[:, j, t, :], iota_e[:, :], eid[:, j, t:t + 1], None, ALU.is_equal))
                tt(msk[:, :, :], eq[:, 0], eq[:, 1], ALU.add).then_inc(S("msk_ready"), 1)
                ve.wait_ge(S("gex_ready"), i + 1)
                link(stt(den[:, :], e21[:, :], 1.0, gsum[:, :], ALU.add, ALU.mult))
                link(ve.reciprocal(wgt[:, 0, :], den[:, :]))
                link(tt(wgt[:, 1, :], e21[:, :], wgt[:, 0, :], ALU.mult))
                for t in range(TT):
                    link(ts(wtok[:, t, :], eq[:, 0, t, :], wgt[:, 0, t:t + 1], None, ALU.mult))
                    link(stt(wtok[:, t, :], eq[:, 1, t, :], wgt[:, 1, t:t + 1], wtok[:, t, :], ALU.mult, ALU.add))
                ve.wait_ge(S("pos_done"), i + 1)
                link(ve.tensor_copy(pos[:, :, :], PS[:, 0, 0:TT * NE].rearrange("p (t n) -> p t n", t=TT)))
                for j in range(2):
                    link(tt(ptmp[:, j], eq[:, j], pos[:, :, :], ALU.mult))
                    link(ve.tensor_reduce(pch[:, j, :], ptmp[:, j], AX.X, ALU.add))
                link(stt(v2[:, :, :], eid[:, :, :], float(CAP), pch[:, :, :], ALU.mult, ALU.add))
                for r in range(1, T // CAP):
                    dst = pr1[:, :, :] if r == 1 else val[:, :, :]
                    link(ts(dst, pch[:, :, :], float(r * CAP), float((NE - 1) * CAP), ALU.is_ge, ALU.mult))
                    link(tt(v2[:, :, :] if r < T // CAP - 1 else slot[:, :, :], v2[:, :, :], dst, ALU.add))
                ve.tensor_reduce(past[:, :], pr1[:, :, :], AX.XY, ALU.add).then_inc(S("past_ready"), 1)
                ve.wait_ge(S("past_ready"), i + 1)

            def select(i, q):
                n = NSTEP_SEL * i + q
                if not (isinstance(n, int) and n == 0):
                    ve.wait_ge(S("sel_used"), NSTEP * i + q)
                for t in range(TT):
                    ts(sel[:, t, :], iota_slot[:, :], slot[:, 0, t:t + 1], None, ALU.is_equal)\
                        .then_inc(S("sel_own"), 1)
                for t in range(TT):
                    ve.wait_ge(S("sel_own"), n * 5 + t + 1)
                    stt(sel[:, t, :], iota_slot[:, :], slot[:, 1, t:t + 1], sel[:, t, :].bitcast(F32), ALU.is_equal,
                        ALU.add).then_inc(S("sel_own"), 1)
                ve.wait_ge(S("sel_own"), n * 5 + 4)
                ts(slot[:, :, :], slot[:, :, :], -float(GS), None, ALU.add).then_inc(S("sel_own"), 1)
                ve.wait_ge(S("sel_own"), n * 5 + 5)

            def chunk(i, g, jj, c):
                n = 4 * NE * i + 4 * GE * g + 4 * jj + c
                s = items[moe_item[i] + jj % GE][0]
                ve.wait_ge(S("hi_ready"), n + 1)
                r = ring[s][:, 0:4096].rearrange("p (u n) -> p u n", u=2)[:, :, 512 * c:512 * c + 512]
                tt(wlo[:, c].rearrange("p k (u f) -> p u k f", u=2), r.rearrange("p u (k f) -> p u k f", k=2),
                   whi[:, c].bitcast(F32).rearrange("p k (u f) -> p u k f", u=2), ALU.subtract)\
                    .then_inc(S("lo_ready"), 1)

            def gather_sum(i, e):
                ve.wait_ge(S("flo_ready"), NE * i + e + 1)
                tt(gu[:, :], PS[0:64, 0, :], flo[:, :], ALU.add).then_inc(S("gu_ready"), 1)

            def gate(i, g, par, jj):
                n = NE * i + GE * g + jj
                ve.wait_ge(S("silu_ready"), n + 1)
                ve.wait_ge(S("gu_ready"), n + 1)
                if jj % GE == 0:
                    ve.wait_ge(S("m_evicted"), WSLOT_M(i, g, jj))
                stt(act[:, :], act[:, :], wslot[0:64, (par + jj // GE) % 2, jj % GE:jj % GE + 1], gu[:, FF:2 * FF],
                    ALU.mult, ALU.mult).then_inc(S("act_ready"), 1)

            def step(i, g, par, j, last):
                e = g * GE + j
                more = not (last and j >= 2)
                nxt = not (last and j == 3)
                if more:
                    chunk(i, g, j + 2, 0)
                    chunk(i, g, j + 2, 1)
                if nxt:
                    gather_sum(i, e + 1)
                if more:
                    chunk(i, g, j + 2, 2)
                if nxt:
                    gate(i, g, par, j + 1)
                if more:
                    chunk(i, g, j + 2, 3)
                if j % 2:
                    pair = g * 2 + j // 2 + NE // 2 * i
                    for n in range(2):
                        ve.wait_ge(S("ohi_ready"), pair * 2 + n + 1)
                        cs = slice(512 * n, 512 * n + 512)
                        tt(olo[:, cs], PS[:, 2 + n, :], ohi[:, cs].bitcast(F32), ALU.subtract)\
                            .then_inc(S("olo_ready"), 1)
                if j == 3 and not last:
                    select(i, g + 2)

            def moe(i):
                norm_scale(1 + 3 * i)
                norm_evict(1 + 3 * i, hT)
                for t in range(TT):
                    ve.tensor_copy(hhi[:, t, :], h[:, t, :]).then_inc(S("hhi_ready"), 1)
                for t in range(TT):
                    ve.wait_ge(S("hhi_ready"), TT * i + t + 1)
                    tt(hlo[:, t, :], h[:, t, :], hhi[:, t, :].bitcast(F32), ALU.subtract).then_inc(S("hlo_ready"), 1)
                route(i)
                select(i, 0)
                for c in range(4):
                    chunk(i, 0, 0, c)
                select(i, 1)
                ve.wait_ge(S("past_done"), i + 1)
                ts(many[:, :], PS[0:1, 3, 0:1], 1.0, None, ALU.min).then_inc(S("many_ready"), 1)
                chunk(i, 0, 1, 0)
                chunk(i, 0, 1, 1)
                gather_sum(i, 0)
                chunk(i, 0, 1, 2)
                gate(i, 0, 0, 0)
                chunk(i, 0, 1, 3)
                for j in range(GE):
                    step(i, 0, 0, j, False)
                with ve.Fori(0, (NSTEP - 2) // 2) as r:
                    for sub in (1, 2):
                        for j in range(GE):
                            step(i, r * 2 + sub, sub % 2, j, False)
                for j in range(GE):
                    step(i, NSTEP - 1, 1, j, True)
                ve.wait_ge(S("comb_done"), NE // 2 * (i + 1))
                for t in range(TT):
                    for c in range(2):
                        xs = x[:, t, 512 * c:512 * c + 512]
                        ins = tt(xs, xs, PS[:, 4 + 2 * t + c, :], ALU.add)
                ins.then_inc(S("x_summed"), 1)
                ve.wait_ge(S("x_summed"), i + 1)

                def more(n):
                    name = lambda what: S(f"ov_{what}{i}")
                    for j in range(2):
                        for t in range(TT):
                            if j == 0:
                                ts(oh_ov[:, t, :], iota_slot[:, 0:CAP], slot[:, 0, t:t + 1], None, ALU.is_equal)\
                                    .then_inc(name("own"), 1)
                            else:
                                stt(oh_ov[:, t, :], iota_slot[:, 0:CAP], slot[:, 1, t:t + 1], oh_ov[:, t, :],
                                    ALU.is_equal, ALU.add).then_inc(name("own"), 1)
                        ve.wait_ge(name("own"), n * 5 + 2 * j + 2)
                    ts(slot[:, :, :], slot[:, :, :], -float(CAP), None, ALU.add).then_inc(name("own"), 1)
                    ve.wait_ge(name("own"), n * 5 + 5)
                    ve.sem_inc(name("sel"), 1)
                    ve.wait_ge(name("gathered"), n + 1)
                    ve.tensor_copy(xo[:, :, :].rearrange("p k j -> p (k j)"), PS[:, 0, :])
                    ve.tensor_copy(selTo[:, :], PS[0:CAP, 1, 0:T])
                    ve.tensor_copy(wso[:, :], PS[0:CAP, 1, T:T + 1]).then_inc(name("x"), 1)
                    ve.wait_ge(name("x"), n + 1)
                    ve.wait_ge(name("silu"), n + 1)
                    stt(acto[:, :], slu[:, :], wso[:, 0:1], PS[0:CAP, 2, FF:2 * FF], ALU.mult, ALU.mult)\
                        .then_inc(name("act"), 1)
                    ve.wait_ge(name("actT"), n + 1)
                    ve.tensor_copy(actTo[:, :, :].rearrange("p k j -> p (k j)"), PS[:, 3, 0:2 * CAP])\
                        .then_inc(name("actTr"), 1)
                    ve.wait_ge(name("down"), n + 1)
                    ve.tensor_copy(oo[:, :].rearrange("p (b n) -> p b n", b=2), PS[0:CAP, 0:2, :]).then_inc(name("o"), 1)
                    ve.wait_ge(name("comb"), n + 1)
                    for t in range(TT):
                        for c in range(2):
                            xs = x[:, t, 512 * c:512 * c + 512]
                            ins = tt(xs, xs, PS[:, 4 + 2 * t + c, :], ALU.add)
                    ins.then_inc(name("added"), 1)
                    ve.wait_ge(name("added"), n + 1)

                link(ts(slot[:, :, :], slot[:, :, :], float(GS), None, ALU.add))
                overflow(ve, i, more)
                ve.sem_inc(S("x_ready"), 1)

            def ple(i):
                norm_scale(2 + 3 * i)
                norm_evict(2 + 3 * i, hT)
                for n in range(4):
                    k = 4 * i + n
                    c, t = divmod(n, 2)
                    b = n % 2
                    ve.wait_ge(S("sg_ready"), k + 1)
                    link(tt(sg[b][:, :], sg[b][:, :], PS[:, 2 * b + 1, :], ALU.mult))
                    xs = x[:, t, 512 * c:512 * c + 512]
                    ins = tt(xs, xs, sg[b][:, :], ALU.add)
                    ins.then_inc(S("ple_used"), 1)
                    ve.wait_ge(S("ple_used"), k + 1)
                ve.sem_inc(S("x_ready") if i == 0 else S("x_out"), 1)

            moe(0)
            ple(0)

            norm_scale(3)
            norm_evict(3, hT)

            def qkv_evict(n):
                ve.wait_ge(S("qkv_done"), n + 1)
                w = n // 2
                dst = qk[:, 1, 8 * w:8 * w + 8, :].rearrange("p a d -> p (a d)") if w < 4 else \
                    vt[:, 1, 512 * (w - 4):512 * (w - 4) + 512]
                ve.tensor_copy(dst, PS[:, n % 4, :]).then_inc(S("qkv_d"), 1)

            for n in (1, 3, 5, 7):
                qkv_evict(n)
            for t in range(TT):
                ve.wait_ge(S("sq_ready"), t + 1)
                ve.tensor_reduce(qss[:, t, :], sq[:, :, :], AX.X, ALU.add).then_inc(S("qss_ready"), 1)
                ve.wait_ge(S("qss_ready"), t + 1)
                ts(qms[:, t, :], qss[:, t, :], 1.0 / HD, EPS, ALU.mult, ALU.add).then_inc(S("qms_ready"), 1)
            qkv_evict(9)
            qkv_evict(11)
            for t in range(TT):
                ve.wait_ge(S("qrs_ready"), t + 1)
                tt(qk[:, t], qk[:, t], bc(qrs[:, t, :], 2, HD), ALU.mult).then_inc(S("qkn_ready"), 1)
            ve.wait_ge(S("qkw_loaded"), 64)
            for t in range(TT):
                for n in range(2):
                    ve.wait_ge(S("k_T"), 2 * t + n + 1)
                    ts(kT[:, 4 * n:4 * n + 4, P * t:P * t + P], PS[:, 6 + n, :].rearrange("p (a t) -> p a t", a=4),
                       qkw[:, 1:2], None, ALU.mult).then_inc(S("kT_ready"), 1)

            def scores(a):
                b = a % 2
                ve.wait_ge(S("bias_ready"), a + 1)
                ve.wait_ge(S("s_done"), a + 1)
                if a >= 2:
                    ve.wait_ge(S("prob_T"), a - 1)
                bi_ = bias[a // (NH // 2)][:, a % (NH // 2)].rearrange("p t r c -> p (t r) c")
                tt(prob[:, b].rearrange("p t (r c) -> p (t r) c", r=ROWS),
                   PS[:, b, :].rearrange("p (r c) -> p r c", c=GW), bi_[:, :, ::-1], ALU.add)\
                    .then_inc(S("sb_ready"), 1)
                ve.wait_ge(S("sb_ready"), a + 1)
                ve.tensor_reduce(mx[:, b, :], prob[:, b], AX.X, ALU.max, negate=True).then_inc(S("mx_ready"), 1)

            def normalise(a):
                b = a % 2
                ve.wait_ge(S("exp_ready"), TT * (a + 1))
                link(ve.reciprocal(rr[:, b, :], rs[:, b, :]))
                for t in range(TT):
                    ts(prob[:, b, t, :], prob[:, b, t, :], rr[:, b, t:t + 1], None, ALU.mult)\
                        .then_inc(S("prob_ready"), 1)

            def out_evict(a):
                ve.wait_ge(S("pv_done"), a + 2)
                ve.tensor_copy(oT[:, a // 2, :], PS[:, 4 + (a // 2) % 2, 0:T]).then_inc(S("oT_ready"), 1)

            for a in range(NH + 3):
                if a < NH:
                    scores(a)
                if 1 <= a <= NH:
                    normalise(a - 1)
                if a >= 4 and a % 2 == 0:
                    out_evict(a - 4)
            for n in range(4):
                c, t = divmod(n, 2)
                ve.wait_ge(S("wo_done"), n + 1)
                xs = x[:, t, 512 * c:512 * c + 512]
                ins = tt(xs, xs, PS[:, 6 + n % 2, :], ALU.add)
                ins.then_inc(S("wo_used"), 1)
            ve.wait_ge(S("wo_used"), 4)
            ve.sem_inc(S("x_ready"), 1)
            moe(1)
            ple(1)

        @block.tensor
        def _(pe):
            mm = pe.matmul

            def norm_T(n):
                for t in range(TT):
                    pe.wait_ge(S("h_ready"), TT * n + t + 1)
                    for kq in range(2):
                        for k in range(4):
                            ins = pe.transpose(PS[:, NB + 2 * t + kq, P * k:P * k + P], h[:, t, 4 * kq + k::KD],
                                               ident[:, :])
                        ins.then_inc(S("h_T2") if t else S("h_T"), 1)
                pe.wait_ge(S("hT_a"), 2 * n + 2)
                pe.wait_ge(S("hT_d"), 2 * n + 2)

            pe.wait_ge(S("ident_ready"), 1)
            pe.wait_ge(S("coef_ready"), 1)
            for n, q in enumerate((0, 2, 11, 12)):
                ins = pe.transpose(PS[:, 0, SG * n:SG * n + SG], pq[:, q], ident[0:SG, 0:SG])
            ins.then_inc(S("prm_T"), 1)
            pe.wait_ge(S("c_loaded"), 64)
            for c in range(2):
                for a in range(4):
                    ins = pe.transpose(PS[:, 1 + c, P * a:P * a + P],
                                       craw[:, c, a].rearrange("p d n -> p (d n)"), ident[:, :])
                ins.then_inc(S("c_T"), 1)
            norm_T(0)
            arrived(pe, IT["w_in"])
            w_in = ring[0][:, 0:KD * SW].rearrange("p (k n) -> p k n", k=KD)
            for a in range(4):
                for k in range(KD):
                    ins = mm(PS[:, 4 + a // 2, T * (a % 2):T * (a % 2) + T], w_in[:, k, P * a:P * a + P],
                             s5hT[:, k, :], start=k == 0, stop=k == KD - 1)
            ins.then_inc(S("u_done"), 1)
            pe.wait_ge(S("u_done"), 1)
            for n in range(SG // 2):
                pe.wait_ge(S("s5W_half"), n // (SG // 4) + 1)
                if n >= 2:
                    pe.wait_ge(S("WT_ready"), n - 1)
                else:
                    pe.wait_ge(S("cT_ready"), 2)
                for gg in range(2):
                    for c in range(2):
                        o_ = 256 * gg + 128 * c
                        ins = pe.transpose(PS[:, 2 + n % 2, o_:o_ + P],
                                           s5W[:, c, 2 * n + gg].rearrange("p l h -> p (l h)"), ident[:, :])
                ins.then_inc(S("W_T"), 1)
            for n in range(SG // 4):
                pe.wait_ge(S("s5V_re"), n // (SG // 8) + 1)
                pe.wait_ge(S("s5V_im"), n // (SG // 8) + 1)
                if n >= 2:
                    pe.wait_ge(S("s5T_ready"), n - 1)
                if n == 1:
                    pe.wait_ge(S("WT_ready"), SG // 2)
                for gg in range(4):
                    for d in range(2):
                        hf = slice(64 * d, 64 * d + 64)
                        for c in range(2):
                            ins = mm(PS[:, 2 * (n % 2) + d, P * gg:P * gg + P],
                                     s5W[hf, c, 4 * n + gg].rearrange("p l h -> p (l h)"),
                                     s5V[hf, c, 4 * n + gg].rearrange("p l h -> p (l h)"), start=c == 0, stop=c == 1)
                        if gg == 3:
                            ins.then_inc(S("T_done"), 1)
            pe.wait_ge(S("us_loaded"), 16 * L)
            pe.wait_ge(S("WT_ready"), SG // 2)
            pe.wait_ge(S("uT_half"), 2)
            for c in range(2):
                for g in range(SG):
                    ins = mm(PS[:, 4 + 2 * c + g // 16, NC_ * (g % 16):NC_ * (g % 16) + NC_], s5WT[:, c, g, :],
                             us[:, g, :], start=True, stop=True)
            ins.then_inc(S("v_done"), 1)
            pe.wait_ge(S("s5T_ready"), SG // 4)
            pe.wait_ge(S("S_ready"), 2)
            for g in range(SG):
                o_ = PS[:, 2 + g // 16, NC_ * (g % 16):NC_ * (g % 16) + NC_]
                mm(o_, s5T[:, g, :], us[:, g, :], start=True, stop=False)
                mm(o_, s5V[:, 0, g].rearrange("p l h -> p (l h)"), sc[4][:, g, :], start=False, stop=False)
                ins = mm(o_, s5V[:, 1, g].rearrange("p l h -> p (l h)"), sc[5][:, g, :], start=False, stop=True)
            ins.then_inc(S("y_done"), 1)
            pe.wait_ge(S("gelu_ready"), 1)
            arrived(pe, IT["w_out"][0])
            arrived(pe, IT["w_out"][1])
            for n in range(4):
                t, c = divmod(n, 2)
                if n >= 2:
                    pe.wait_ge(S("glu_used"), n - 1)
                for w in range(2):
                    wv = ring[w][:, 0:4 * D].rearrange("p (k n) -> p k n", k=4)
                    for k in range(4):
                        ins = mm(PS[:, 4 + 2 * (n % 2) + w, :], yT[4][:, k, P * t:P * t + P],
                                 wv[:, k, 512 * c:512 * c + 512], start=k == 0, stop=k == 3)
                ins.then_inc(S("glu_done"), 1)

            def gather_up(i, g, par, jj):
                n = NE * i + GE * g + jj
                if not (isinstance(n, int) and n == 0):
                    pe.wait_ge(S("gu_ready"), n)
                p_ = (par + jj // GE) % 2
                for c in range(4):
                    pe.wait_ge(S("lo_ready"), n * 4 + c + 1)
                    for k in range(2):
                        for w, half in enumerate((wlo, whi)):
                            ins = mm(PS[:, 0, :], xg[:, p_, jj % GE, 2 * c + k].rearrange("p c j -> p (c j)"),
                                     half[:, c, k, :], start=(c, k, w) == (0, 0, 0), stop=(c, k, w) == (3, 1, 1))
                    if c < 3:
                        ins.then_inc(S("split_used"), 1)
                ins.then_inc(S("split_used"), 1)
                pe.wait_ge(S("split_used"), n * 4 + 4)
                pe.sem_inc(S("gu_done"), 1)

            def bank1(m):
                if not (isinstance(m, int) and m == 0):
                    pe.wait_ge(S("m_evicted"), m)

            def units(i, g, par, lst, m):
                for n, u in enumerate(lst):
                    bank1(m + n)
                    if u == "selT":
                        pe.wait_ge(S("sel_own"), (NSTEP_SEL * i + g) * 5 + 4)
                        for pr_ in range(2):
                            for t in range(TT):
                                ins = pe.transpose(PS[:, 1, T * pr_ + P * t:T * pr_ + P * t + P],
                                                   sel[:, t, P * pr_:P * pr_ + P].bitcast(F32), ident[:, :])
                    elif u == "wslot":
                        for e in range(GE):
                            for t in range(TT):
                                ins = mm(PS[0:64, 1, e:e + 1], sel[:, t, CAP * e:CAP * e + CAP].bitcast(F32),
                                         wtok[:, t, bass.ds(g * GE + e, 1)], start=t == 0, stop=t == 1)
                    else:
                        for c, half in enumerate((hhi, hlo)):
                            for t in range(TT):
                                ins = mm(PS[:, 1, GS * c:GS * c + GS], half[:, t, u::KD], sel[:, t, :],
                                         start=t == 0, stop=t == 1)
                    ins.then_inc(S("m_written"), 1)
                    if u == 7:
                        pe.wait_ge(S("m_written"), m + n + 1)
                        pe.sem_inc(S("sel_used"), 1)

            def down(i, g, j, n, s):
                rows = slice(CAP * (j % 2), CAP * (j % 2) + CAP)
                wd = ring[s][:, 4096:6144].rearrange("p (k n) -> p k n", k=2)
                for k in range(2):
                    ins = mm(PS[rows, 2 + n, :], actT[:, k, :], wd[:, k, 512 * n:512 * n + 512],
                             start=k == 0, stop=k == 1)
                return ins

            def combine(i, pair, spar, pr_, first, last):
                for n in range(2):
                    pe.wait_ge(S("olo_ready"), pair * 2 + n + 1)
                    for t in range(TT):
                        for w, half in enumerate((ohi, olo)):
                            ins = mm(PS[:, 4 + 2 * t + n, :], selT[:, spar, pr_, P * t:P * t + P],
                                     half[:, 512 * n:512 * n + 512], start=first and w == 0, stop=last and w == 1)
                ins.then_inc(S("comb_done"), 1)

            def step(i, g, par, j, last):
                e = NE * i + GE * g + j
                m = M_BASE * i + 10 + 14 * g
                mt = m + (j if last else M_POS[j][0])
                s = items[moe_item[i] + j][0]
                pe.wait_ge(S("act_ready"), e + 1)
                bank1(mt)
                for k in range(2):
                    ins = mm(PS[:, 1, CAP * k:CAP * k + CAP], act[:, k::2], ident[0:CAP, 0:CAP], start=True, stop=True)
                ins.then_inc(S("m_written"), 1)
                if not (last and j == 3):
                    gather_up(i, g, par, j + 1)
                if j % 2 == 0:
                    pair = NE // 2 * i + g * 2 + j // 2 - 1
                    if not (isinstance(g, int) and g == 0 and j == 0):
                        first = isinstance(g, int) and g == 0 and j == 2
                        combine(i, pair, (par - (j == 0)) % 2, 1 - j // 2, first, False)
                if not last:
                    units(i, g + 1, 1 - par, UNITS[j][0], m + M_POS[j][1])
                pe.wait_ge(S("m_evicted"), mt + 1)
                if j % 2 == 0:
                    pair = NE // 2 * i + g * 2 + j // 2
                    if not (isinstance(pair, int) and pair == 0):
                        pe.wait_ge(S("olo_ready"), pair * 2)
                down(i, g, j, 0, s)
                if not last:
                    units(i, g + 1, 1 - par, UNITS[j][1], m + M_POS[j][2])
                down(i, g, j, 1, s).then_inc(S("d_done"), 1)

            def moe(i):
                norm_T(1 + 3 * i)
                pe.wait_ge(S("router_loaded"), 64 * (i + 1))
                for t in range(TT):
                    for k in range(KD):
                        ins = mm(PS[:, 0, (NG + NE) * t:(NG + NE) * (t + 1)], hT[:, k, P * t:P * t + P], wr[:, k, :],
                                 start=k == 0, stop=k == KD - 1)
                ins.then_inc(S("logits_done"), 1)
                pe.wait_ge(S("msk_ready"), i + 1)
                mm(PS[:, 0, 0:NE], tri[:, :], msk[:, 0], start=True, stop=True)
                mm(PS[:, 0, NE:2 * NE], ones[:, :], msk[:, 0], start=True, stop=False)
                mm(PS[:, 0, NE:2 * NE], tri[:, :], msk[:, 1], start=False, stop=True).then_inc(S("pos_done"), 1)
                pe.wait_ge(S("hhi_ready"), TT * (i + 1))
                pe.wait_ge(S("hlo_ready"), TT * (i + 1))
                units(i, 0, 0, ALL_UNITS, M_BASE * i)
                pe.wait_ge(S("m_evicted"), M_BASE * i + 10)
                pe.wait_ge(S("past_ready"), i + 1)
                mm(PS[0:1, 3, 0:1], past[:, :], ones[:, 0:1], start=True, stop=True).then_inc(S("past_done"), 1)
                gather_up(i, 0, 0, 0)
                for j in range(GE):
                    step(i, 0, 0, j, False)
                with pe.Fori(0, (NSTEP - 2) // 2) as r:
                    for sub in (1, 2):
                        for j in range(GE):
                            step(i, r * 2 + sub, sub % 2, j, False)
                for j in range(GE):
                    step(i, NSTEP - 1, 1, j, True)
                combine(i, NE // 2 * (i + 1) - 1, 1, 1, False, True)

                def more(n):
                    name = lambda what: S(f"ov_{what}{i}")
                    pe.wait_ge(name("sel"), n + 1)
                    for k in range(KD):
                        for q, half in enumerate((hhi, hlo)):
                            for t in range(TT):
                                mm(PS[:, 0, CAP * k:CAP * k + CAP], half[:, t, k::KD].bitcast(F32), oh_ov[:, t, :],
                                   start=(q, t) == (0, 0), stop=(q, t) == (1, 1))
                    for t in range(TT):
                        mm(PS[0:CAP, 1, P * t:P * t + P], oh_ov[:, t, :], ident[:, :], start=True, stop=True)
                    for t in range(TT):
                        ins = mm(PS[0:CAP, 1, T:T + 1], oh_ov[:, t, :], wtok[:, t, bass.ds(n % NE, 1)],
                                 start=t == 0, stop=t == 1)
                    ins.then_inc(name("gathered"), 1)
                    s = items[moe_item[i]][0]
                    pe.wait_ge(S(f"ov_loaded{i}"), n * 48 + 48)
                    pe.wait_ge(name("x"), n + 1)
                    wv = ring[s][:, 0:4096].rearrange("p (u k f) -> p u k f", u=2, k=KD)
                    for u in range(2):
                        for k in range(KD):
                            ins = mm(PS[0:CAP, 2, FF * u:FF * u + FF], xo[:, k, :], wv[:, u, k, :],
                                     start=k == 0, stop=k == KD - 1)
                    ins.then_inc(name("gu"), 1)
                    pe.wait_ge(name("act"), n + 1)
                    for k in range(2):
                        ins = mm(PS[:, 3, CAP * k:CAP * k + CAP], acto[:, k::2], ident[0:CAP, 0:CAP],
                                 start=True, stop=True)
                    ins.then_inc(name("actT"), 1)
                    pe.wait_ge(name("actTr"), n + 1)
                    wd = ring[s][:, 4096:6144].rearrange("p (k n) -> p k n", k=2)
                    for c in range(2):
                        for k in range(2):
                            ins = mm(PS[0:CAP, c, :], actTo[:, k, :], wd[:, k, 512 * c:512 * c + 512],
                                     start=k == 0, stop=k == 1)
                    ins.then_inc(name("down"), 1)
                    pe.wait_ge(name("down"), n + 1)
                    pe.sem_inc(name("free"), 1)
                    pe.wait_ge(name("o"), n + 1)
                    for t in range(TT):
                        for c in range(2):
                            ins = mm(PS[:, 4 + 2 * t + c, :], selTo[:, P * t:P * t + P], oo[:, 512 * c:512 * c + 512],
                                     start=True, stop=True)
                    ins.then_inc(name("comb"), 1)

                overflow(pe, i, more)

            def ple(i):
                norm_T(2 + 3 * i)
                ga, pj, gb = IT["ple"][i]
                sa, sp_, sb = items[ga][0], items[pj][0], items[gb][0]
                arrived(pe, pj)
                pv = ring[sp_][:, 2048:2560].rearrange("p (t n) -> p t n", t=TT)
                for k in range(2):
                    for t in range(TT):
                        ins = pe.transpose(PS[:, 0, T * k + P * t:T * k + P * t + P], pv[:, t, k::2], ident[:, :])
                ins.then_inc(S("p_T"), 1)
                pe.wait_ge(S("pT_ready"), i + 1)
                wp_v = ring[sp_][:, 0:2048].rearrange("p (k n) -> p k n", k=2)
                for n in range(4):
                    c, t = divmod(n, 2)
                    b = 2 * (n % 2)
                    if t == 0:
                        arrived(pe, gb if c else ga)
                    wg = ring[sb if c else sa][:, 0:4096].rearrange("p (k n) -> p k n", k=KD)
                    if n >= 2:
                        pe.wait_ge(S("ple_used"), 4 * i + n - 1)
                    for k in range(2):
                        mm(PS[:, b + 1, :], pT[:, k, P * t:P * t + P], wp_v[:, k, 512 * c:512 * c + 512],
                           start=k == 0, stop=k == 1)
                    for k in range(KD):
                        ins = mm(PS[:, b, :], hT[:, k, P * t:P * t + P], wg[:, k, :], start=k == 0, stop=k == KD - 1)
                    ins.then_inc(S("ple_done"), 1)

            moe(0)
            ple(0)

            norm_T(3)
            for n in range(12):
                w, t = divmod(n, 2)
                if t == 0:
                    arrived(pe, IT["qkv"][w])
                if n >= 4:
                    pe.wait_ge(S("qkv_d") if t else S("qkv_a"), n // 2 - 1)
                wv = ring[items[IT["qkv"][w]][0]][:, 0:4096].rearrange("p (k n) -> p k n", k=KD)
                for k in range(KD):
                    ins = mm(PS[:, n % 4, :], hT[:, k, P * t:P * t + P], wv[:, k, :], start=k == 0, stop=k == KD - 1)
                ins.then_inc(S("qkv_done"), 1)
            for t in range(TT):
                pe.wait_ge(S("qkn_ready"), t + 1)
                for b, what in ((4, "q_T"), (6, "k_T")):
                    for n in range(2):
                        if t:
                            pe.wait_ge(S("qT_ready") if b == 4 else S("kT_ready"), n + 1)
                        for a in range(4):
                            hd = (0 if b == 4 else NH) + 2 * (4 * n + a)
                            ins = pe.transpose(PS[:, b + n, P * a:P * a + P],
                                               qk[:, t, hd:hd + 2, :].rearrange("p a d -> p (a d)"), ident[:, :])
                        ins.then_inc(S(what), 1)
            pe.wait_ge(S("qT_ready"), 4)
            pe.wait_ge(S("kT_ready"), 4)
            pe.wait_ge(S("qkv_a"), 6)
            pe.wait_ge(S("qkv_d"), 6)

            def scores(a):
                if a >= 2:
                    pe.wait_ge(S("sb_ready"), a - 1)
                r = slice(64 * (a % 2), 64 * (a % 2) + 64)
                for t in range(TT):
                    ins = mm(PS[:, a % 2, T * t:T * t + T], qT[r, a // 2, P * t:P * t + P], kT[r, a // 2, :],
                             start=True, stop=True)
                ins.then_inc(S("s_done"), 1)

            def prob_T(a):
                pe.wait_ge(S("prob_ready"), TT * (a + 1))
                if a >= 2:
                    pe.wait_ge(S("probT_ready"), a - 1)
                for kt in range(2):
                    for t in range(TT):
                        ins = pe.transpose(PS[:, 2 + a % 2, T * kt + P * t:T * kt + P * t + P],
                                           prob[:, a % 2, t, P * kt:P * kt + P], ident[:, :])
                ins.then_inc(S("prob_T"), 1)

            def values(a):
                pe.wait_ge(S("probT_ready"), a + 1)
                if a >= 4 and a % 2 == 0:
                    pe.wait_ge(S("oT_ready"), a // 2 - 1)
                r = slice(64 * (a % 2), 64 * (a % 2) + 64)
                for kt in range(2):
                    ins = mm(PS[r, 4 + (a // 2) % 2, 0:T], vt[:, kt, HD * a:HD * a + HD], probT[:, a % 2, kt, :],
                             start=kt == 0, stop=kt == 1)
                ins.then_inc(S("pv_done"), 1)

            for a in range(NH + 2):
                if a < NH:
                    scores(a)
                if 1 <= a <= NH:
                    prob_T(a - 1)
                if a >= 2:
                    values(a - 2)
            pe.wait_ge(S("oT_ready"), NH // 2)
            for n in range(4):
                c, t = divmod(n, 2)
                if t == 0:
                    arrived(pe, IT["wo"][c])
                if n >= 2:
                    pe.wait_ge(S("wo_used"), n - 1)
                wv = ring[items[IT["wo"][c]][0]][:, 0:4096].rearrange("p (k n) -> p k n", k=KD)
                for k in range(KD):
                    ins = mm(PS[:, 6 + n % 2, :], oT[:, k, P * t:P * t + P], wv[:, k, :], start=k == 0, stop=k == KD - 1)
                ins.then_inc(S("wo_done"), 1)
            moe(1)
            ple(1)


_INS = ["x", "p", "norm_mix", "norm_ffn", "norm_ple", "s5_w_in", "s5_lam_re", "s5_lam_im", "s5_log_dt",
        "s5_b_re", "s5_b_im", "s5_c_re", "s5_c_im", "s5_d", "s5_w_out", "nat_w_qkv", "nat_q_norm", "nat_k_norm",
        "nat_rpb", "nat_w_o", "moe_w_group", "moe_b_group", "moe_w_expert", "moe_b_expert", "moe_w_gate",
        "moe_w_up", "moe_w_down", "ple_w_proj", "ple_w_gate"]


def kernel(**inputs):
    import numpy as np
    import concourse.bacc as bacc
    from concourse.bass_utils import run_bass_kernel_spmd

    nc = bacc.Bacc("TRN2", target_bir_lowering=False, num_devices=1)
    arrays, views = {}, {}
    for name in _INS:
        a = np.ascontiguousarray(inputs[name])
        arrays[f"in_{name}"] = a
        views[name] = nc.dram_tensor(f"in_{name}", a.shape, mybir.dt.from_np(a.dtype), kind="ExternalInput").ap()
    out = nc.dram_tensor("out_0", (1, T, D), F32, kind="ExternalOutput").ap()
    program(nc, views, out)
    r = run_bass_kernel_spmd(nc, [arrays], core_ids=[0])
    return r.results[0]["out_0"]
```

```python
import math
from contextlib import ExitStack

import concourse.bass as bass
from concourse import mybir

F32 = mybir.dt.float32
F32R = mybir.dt.float32r
U32 = mybir.dt.uint32
I32 = mybir.dt.int32
ALU = mybir.AluOpType
ACT = mybir.ActivationFunctionType
AX = mybir.AxisListType

P = 128
D = 1024
T = 256
TT = T // P
KD = D // P
EPS = 1e-6
SG, SH, SP_ = 32, 16, 64
SW = SG * SH
L = 8
NC_ = T // L
NH, HD, GW, ROWS = 16, 64, 64, 4
WR, WC = 8, 16
MASKV = -1e30
NG, EG = 4, 8
NE = NG * EG
FF = 256
CAP = 64
GE = 4
GS = GE * CAP
NSTEP = NE // GE
MAGIC = 12582912.0
TWO_PI_HI = 6.28125
TWO_PI_LO = 2 * math.pi - 6.28125
TURN = 6.2831850


def bc(ap, axis, n):
    dims = [list(d) for d in ap.ap]
    dims.insert(axis, [0, n])
    return bass.AP(ap.tensor, ap.offset, dims)


def program(nc, I, out):
    ctx = ExitStack()
    with ctx:
        sems = {}

        def S(name):
            if name not in sems:
                sems[name] = ctx.enter_context(nc.semaphore(name))
            return sems[name]

        base = 16512
        addr = [base]

        def at(name, shape, dtype, off):
            return nc.alloc_sbuf_tensor_at(name, shape, dtype, offset=off)

        def new(name, shape, dtype=F32):
            n = 4
            for s in shape[1:]:
                n *= s
            n = (n + 31) // 32 * 32
            t = at(name, shape, dtype, addr[0])
            addr[0] += n
            return t

        ident = new("ident", [P, P])
        tri = new("tri", [P, P])
        mhalf = new("mhalf", [P, 32])
        ones = new("ones", [P, P])
        iota_slot = new("iota_slot", [P, GS])
        iota_i = at("iota_i", [P, GS], I32, base + 160000)
        iota_e = new("iota_e", [P, NE])
        negh = new("negh", [P, 64])
        ss = new("ss", [P, 4])
        ms = new("ms", [P, 4])
        rstd = new("rstd", [P, 4])
        slot = new("slot", [P, 2, TT])
        wtok = new("wtok", [P, TT, NE])
        wslot = new("wslot", [P, 2, GE])
        many = new("many", [1, 1], I32)
        dskip = new("dskip", [P, SW // P])
        assert addr[0] <= base + 4096, addr[0] - base
        A0 = base + 4096
        x = at("x", [P, TT, D], F32, A0)
        A_H = A0 + 8192
        hhi = at("hhi", [P, TT, D], F32R, A_H)
        hlo = at("hlo", [P, TT, D], F32R, A_H + 8192)
        A_XG = A_H + 16384
        xg = at("xg", [P, 2, GE, KD, 2, CAP], F32R, A_XG)
        hT = at("hT", [P, KD, T], F32, A_XG)
        A_HI = A_XG + 32768
        whi = at("whi", [P, 4, 2, 2 * FF], F32R, A_HI)
        wlo = at("wlo", [P, 4, 2, 2 * FF], F32R, A_HI + 16384)
        A_O = A_HI + 32768
        ohi = at("ohi", [P, D], F32R, A_O)
        olo = at("olo", [P, D], F32R, A_O + 4096)
        h = at("h", [P, TT, D], F32, A_O)
        A_S = A_O + 8192
        sel = at("sel", [P, TT, GS], F32R, A_S)
        selT = at("selT", [P, 2, 2, T], F32R, A_S + 2048)
        gain_s = at("gain_s", [P, D], F32, A_S)
        gain_hi = at("gain_hi", [P, D], F32, A_HI)
        A_W = A_S + 2048 + 4096
        gu = at("gu", [64, 2 * FF], F32, A_W)
        act = at("act", [64, FF], F32, A_W + 4096)
        actT = at("actT", [P, 2, 2, 2 * CAP], F32, A_W + 2048)
        A_R = A_W + 5632
        RS = 6144
        assert A_R + 4 * RS * 4 <= 229368
        ring = [at(f"ring{s}", [P, RS], F32, A_R + s * RS * 4) for s in range(4)]
        PS = ctx.enter_context(nc.psum_tensor("PS", [P, 8, 512], F32))
        rpbr = nc.dram_tensor("rpbr", (NH * (2 * WR - 1), 2 * WC - 1), F32, kind="Internal").ap()
        ud = nc.dram_tensor("ud", (SW, T), F32, kind="Internal").ap()

        def kp(w, k):
            return w.rearrange("(p k) n -> p k n", k=k)

        items = []

        def item(s, *parts):
            items.append((s, parts))
            return len(items) - 1

        IT = {}
        IT["w_in"] = item(0, (0, kp(I["s5_w_in"][0], KD)))
        wo_s5 = I["s5_w_out"][0].rearrange("(k p) n -> p k n", p=P)
        IT["w_out"] = [item(0, (0, wo_s5[:, :, 0:D])), item(1, (0, wo_s5[:, :, D:2 * D]))]
        moe_item = []

        def moe_items(i, s0):
            moe_item.append(len(items))
            for e in range(NE):
                g, j = divmod(e, EG)
                item((e + s0) % 4,
                     (0, I["moe_w_gate"][i, g, j].rearrange("(p k) n -> p (k n)", k=KD)),
                     (2048, I["moe_w_up"][i, g, j].rearrange("(p k) n -> p (k n)", k=KD)),
                     (4096, I["moe_w_down"][i, g, j].rearrange("(p k) n -> p (k n)", k=2)))

        def ple_items(i, s0):
            wg = kp(I["ple_w_gate"][i], KD)
            a = item(s0 % 4, (0, wg[:, :, 0:512]))
            b = item((s0 + 1) % 4, (0, I["ple_w_proj"][i].rearrange("(p k) n -> p (k n)", k=2)),
                     (2048, I["p"][i, 0, 0:P, :]), (2048 + 256, I["p"][i, 0, P:T, :]))
            c = item((s0 + 2) % 4, (0, wg[:, :, 512:1024]))
            return (a, b, c)

        moe_items(0, 2)
        IT["ple"] = [ple_items(0, 2)]
        wq = kp(I["nat_w_qkv"][0], KD)
        IT["qkv"] = [item((1 + n) % 4, (0, wq[:, :, 512 * n:512 * n + 512])) for n in range(6)]
        wo = I["nat_w_o"][0].rearrange("(k p) n -> p k n", p=P)
        IT["wo"] = [item((3 + n) % 4, (0, wo[:, :, 512 * n:512 * n + 512])) for n in range(2)]
        moe_items(1, 1)
        IT["ple"].append(ple_items(1, 1))
        prev, nth, last, cnt = [], [], {}, {}
        for n, (s, _) in enumerate(items):
            prev.append(last.get(s))
            last[s] = n
            cnt[s] = cnt.get(s, 0) + 1
            nth.append(cnt[s])

        dense = [IT["ple"][0][0], IT["ple"][0][2]] + IT["qkv"] + [IT["ple"][1][0], IT["ple"][1][2]]
        done = {IT["w_in"]: ("u_done", 1)}
        done.update({n: ("glu_done", 4) for n in IT["w_out"]})
        for i in range(2):
            done.update({moe_item[i] + e: ("d_done", NE * i + e + 1) for e in range(NE)})
            done.update({n: ("split_done", 4 * dense.index(n if n in dense else IT["ple"][i][0]) + 4)
                         for n in IT["ple"][i]})
        done.update({n: ("split_done", 4 * dense.index(n) + 4) for n in IT["qkv"]})
        done.update({n: ("wo_done", 2 * c + 2) for c, n in enumerate(IT["wo"])})
        loaded = [S(f"slot_loaded{s}") for s in range(4)]

        def arrived(eng, n):
            eng.wait_ge(loaded[items[n][0]], 48 * nth[n])

        def expert_loaded(i, g, jj):
            return (g + (nth[moe_item[i] + jj % GE] + jj // GE)) * 48

        UNITS = [([0], [1], [2]),
                 ([3], [4], [5]),
                 ([6], [7], ["weights"]),
                 (["selT"], [], [])]
        ALL_UNITS = ["selT"] + list(range(KD - 3)) + ["weights"] + list(range(KD - 3, KD))
        M_FIRST = len(ALL_UNITS)
        FIRST_BANKS = (1, 4, 5, 6, 7)
        M_POS, m_ = [], 0
        for lists in UNITS:
            at_ = [m_, m_ + 1]
            for lst in lists:
                at_.append(at_[-1] + len(lst))
            M_POS.append(at_)
            m_ = at_[-1]
        M_STEP = m_
        M_BASE = M_FIRST + M_STEP * (NSTEP - 1) + GE
        NSTEP_SEL = NSTEP + 1
        W_AT = M_POS[2][3]
        SELT_AT = M_POS[3][1]

        def use(i, g, off):
            return M_BASE * i + M_FIRST + M_STEP * g + off

        def WSLOT_M(i, g, jj):
            if isinstance(g, int) and g * GE + jj < GE:
                return M_BASE * i + M_FIRST
            return use(i, g + (jj // GE - 1), W_AT) + 1

        block = ctx.enter_context(nc.Block())

        gains = [I["norm_mix"][0], I["norm_ffn"][0], I["norm_ple"][0],
                 I["norm_mix"][1], I["norm_ffn"][1], I["norm_ple"][1]]


        def gain_of(n):
            if n % 3 == 2:
                return gain_hi, S("gain_hi_loaded"), 16 * (n // 3 + 1)
            return gain_s, S("gain_s_loaded"), 16 * (n // 3 * 2 + n % 3 + 1)

        O1 = A_R + RS * 4
        s5W = at("s5W", [P, 2, SG, L, SH], F32, A_XG)
        s5V = at("s5V", [P, 2, SG, L, SH], F32, A_HI)
        s5WT = at("s5WT", [P, 2, SG, P], F32, A_R + 2 * RS * 4)
        s5T = at("s5T", [P, SG, P], F32, A_R + 2 * RS * 4 + 32768)
        ct = [at(f"ct{n}", [P, SG, NC_], F32, A_O + 4096 * n) for n in range(2)]
        s5hT = at("s5hT", [P, KD, T], F32, A_H)
        uT = at("uT", [P, SW // P, L, NC_], F32, A_H)
        us = at("us", [P, SG, NC_], F32, A_H + 4096)
        ct0, ct1 = ct
        tmpD = at("tmpD", [P, SG // 2, L, SH], F32, A_R + 2 * RS * 4 + 32768)
        tmpP = at("tmpP", [P, SG // 2, L, SH], F32, A_R + 2 * RS * 4 + 40960)
        tmsk = at("tmsk", [P, 2, 4, P], F32, A_S)
        braw = at("braw", [P, 2, SG, SH], F32, A_H + 8192)
        bbar = at("bbar", [P, 2, SG, SH], F32, A_H + 8192 + 4096)
        stab = at("stab", [P, SG, NC_], F32, A_H + 8192)
        ctab = at("ctab", [P, SG, NC_], F32, A_W)
        rp = at("rp", [NH * (2 * WR - 1) // 2, 2, 2 * WC - 1], F32, A_W + 4096)
        rpf = at("rpf", [NH * (2 * WR - 1) // 2, 2, 2 * WC - 1], F32, A_W + 4352)
        dec = at("dec", [P, SG, NC_], F32, O1 + 16384)
        craw = at("craw", [P, 2, 4, 2, SP_], F32, A_R + 16384)
        cT = at("cT", [P, 2, SG, SH], F32, A_R + 16384 + 4096)
        mask = at("mask", [P, 2, P], F32, A_S + 4096)
        lam = at("lam", [SG, 2, 2, SP_], F32, O1)
        ldt = at("ldt", [SG, 2], F32, O1 + 1024)
        dtt = at("dtt", [SG, 2], F32, O1 + 1056)
        pq = at("pq", [SG, 14, 2 * SP_], F32, O1 + 1088)
        prmT = at("prmT", [P, 4, SG], F32, O1 + 8256)
        wp_i = at("wp_i", [P, L], I32, O1 + 8768)
        wp = at("wp", [P, L], F32, O1 + 8800)
        cidx_i = at("cidx_i", [P, NC_], I32, O1 + 8832)
        cidx = at("cidx", [P, NC_], F32, O1 + 8960)
        t32 = at("t32", [P, 4, SG], F32, O1 + 9088)
        pw = at("pw", [P, 8, SG, L], F32, O1 + 9600)
        sc = [at(f"sc{n}", [P, SG, NC_], F32, a_) for n, a_ in
              enumerate((A_R + 16384, A_R + 20480, A_O, A_O + 4096, A_H + 12288, O1 + 20480))]
        ys = [at(f"ys{n}", [NC_, L, 8, SH], F32, A_XG + 24576 + 4096 * n) for n in range(2)]
        yT = [at(f"yT{n}", [P, SW // P, T], F32, A_XG + 4096 * n) for n in range(5)]
        glu = [at(f"glu{n}", [P, 512], F32, A_XG + 20480 + 2048 * n) for n in range(2)]

        RX = A_XG + 16384
        wr = at("wr", [P, KD, NG + NE], F32, A_W + 4096)
        rbias = at("rbias", [P, NG + NE], F32, A_W + 5248)
        gl = at("gl", [P, TT, 8], F32, RX + 1312)
        el = at("el", [P, TT, NE], F32, RX + 1376)
        gmx = at("gmx", [P, TT, 8], F32, RX + 1632)
        gix = at("gix", [P, TT, 8], U32, RX + 1696)
        gf = at("gf", [P, TT], F32, RX + 1760)
        oh = at("oh", [P, TT, NG], F32, RX + 1792)
        eo = at("eo", [P, TT, NE], F32, RX + 1824)
        ch = at("ch", [P, TT, EG], F32, RX + 2080)
        emx = at("emx", [P, TT, 8], F32, RX + 2144)
        eix = at("eix", [P, TT, 8], U32, RX + 2208)
        ef = at("ef", [P, 2, TT], F32, RX + 2272)
        eid = at("eid", [P, 2, TT], F32, RX + 2304)
        gex = at("gex", [P, TT, NG], F32, RX + 2336)
        gsum = at("gsum", [P, TT], F32, RX + 2368)
        dlt = at("dlt", [P, TT], F32, RX + 2400)
        e21 = at("e21", [P, TT], F32, RX + 2432)
        wgt = at("wgt", [P, 2, TT], F32, RX + 2464)
        ngm = at("ngm", [P, TT], F32, RX + 2496)
        eq = at("eq", [P, 2, TT, NE], F32, RX + 2528)
        msk = at("msk", [P, TT, NE], F32, RX + 3040)
        pos = at("pos", [P, TT, NE], F32, RX + 3296)
        ptmp = at("ptmp", [P, 2, TT, NE], F32, RX + 3552)
        pch = at("pch", [P, 2, TT], F32, RX + 4064)
        val = at("val", [P, 2, TT], F32, RX + 4096)
        v2 = at("v2", [P, 2, TT], F32, RX + 4128)
        den = at("den", [P, TT], F32, RX + 4160)

        qk = at("qk", [P, TT, 2 * NH, HD], F32, A_HI)
        vt = at("vt", [P, TT, D], F32, A_HI + 16384)
        sq = at("sq", [P, 2 * NH, HD], F32, A_HI + 24576)
        qss = at("qss", [P, TT, 2 * NH], F32, A_W)
        qms = at("qms", [P, TT, 2 * NH], F32, A_W + 256)
        qrs = at("qrs", [P, TT, 2 * NH], F32, A_W + 512)
        qkw = at("qkw", [P, 2], F32, A_W + 1024)
        qT = at("qT", [P, NH // 2, T], F32, A_XG + 16384)
        kT = at("kT", [P, NH // 2, T], F32, A_XG + 24576)
        oT = at("oT", [P, NH // 2, T], F32, A_O)
        bias = [at("bias_a", [P, NH // 2, TT, ROWS, GW], F32, A_H),
                at("bias_b", [P, NH // 2, TT, ROWS, GW], F32, A_HI)]
        prob = at("prob", [P, 4, TT, T], F32, A_XG)
        probT = at("probT", [P, 2, 2, T], F32, A_XG + 8192)
        qkw8 = at("qkw8", [P, 1], F32, A_W + 1152)
        mx = at("mx", [P, 4, TT], F32, A_W + 1056)
        rs = at("rs", [P, 4, TT], F32, A_W + 1088)
        rr = at("rr", [P, 4, TT], F32, A_W + 1120)
        hTh = at("hTh", [P, KD, T], F32R, A_XG)
        hTl = at("hTl", [P, KD, T], F32R, A_XG + 8192)
        dwh = at("dwh", [P, 4, 2, 512], F32R, A_XG + 16384)
        ringr = [at(f"ringr{s}", [P, KD, 512], F32R, A_R + s * RS * 4) for s in range(4)]
        SPLIT = {2: 0, 3: 1, 5: 2}
        PLAIN = {0: 0, 1: 1, 4: 2}

        def dense_w(n, c):
            s = items[n][0]
            return (ring[s][:, 1024 * c:1024 * c + 1024].rearrange("p (k n) -> p k n", k=2),
                    ringr[s][:, 2 * c:2 * c + 2, :])

        pT = at("pT", [P, 2, T], F32, A_H)
        sg = [at(f"sg{n}", [P, 512], F32, A_H + 2048 + 2048 * n) for n in range(2)]
        pr = [at(f"pr{n}", [P, 512], F32, A_H + 6144 + 2048 * n) for n in range(2)]

        oh_ov = at("oh_ov", [P, TT, CAP], F32, A_S)
        xo = at("xo", [P, KD, CAP], F32, A_XG)
        selTo = at("selTo", [CAP, T], F32, A_XG + 2048)
        oo = at("oo", [CAP, D], F32, A_XG + 4096)
        slu = at("slu", [CAP, FF], F32, A_XG + 8192)
        wso = at("wso", [CAP, 1], F32, A_XG + 9216)
        acto = at("acto", [CAP, FF], F32, A_XG + 9248)
        actTo = at("actTo", [P, 2, CAP], F32, A_XG + 10272)
        pr1 = at("pr1", [P, 2, TT], F32, RX + 4192)
        past = at("past", [P, 1], F32, RX + 4224)
        NOV = (T // CAP - 1) * NE

        def overflow(eng, i, body, first=None, last=None):
            eng.wait_ge(S("many_ready"), i + 1)
            with eng.If(eng.value_load(many[0:1, 0:1], min_val=0, max_val=2 * T) > 0):
                if first:
                    first()
                with eng.Fori(0, NOV) as n:
                    body(n)
                if last:
                    last()

        SB = (0, 1, 6)

        def seq(eng, sem):
            n = [0]

            def link(ins):
                n[0] += 1
                ins.then_inc(sem, 1)
                eng.wait_ge(sem, n[0])
            return link

        NB = 4

        @block.sync
        def _(sp):
            def load(n):
                s, parts = items[n]
                if prev[n] is not None:
                    name, value = done[prev[n]]
                    sp.wait_ge(S(name), value)
                for j, (c, src) in enumerate(parts):
                    w = 1
                    for m in src.shape[1:]:
                        w *= m
                    dst = ring[s][:, c:c + w]
                    if len(src.shape) == 3:
                        dst = dst.rearrange("p (k n) -> p k n", k=src.shape[1])
                    sp.dma_start(dst, src).then_inc(loaded[s], 48 - 16 * (len(parts) - 1) if j == 0 else 16)

            sp.wait_ge(S("lam_loaded"), 48)
            sp.dma_start(x[:, :, :], I["x"][0].rearrange("(a p) d -> p a d", p=P)).then_inc(S("x_loaded"), 16)
            load(IT["w_in"])
            sp.wait_ge(S("uT_half"), 2)
            sp.dma_start(ud.rearrange("(k p) t -> p k t", p=P),
                         uT[:, :, :, :].rearrange("p k s c -> p k (s c)")).then_inc(S("ud_written"), 16)
            sp.wait_ge(S("ud_written"), 16)
            uv = ud.rearrange("(g h) (s c) -> s h g c", h=SH, s=L)
            for s in range(L):
                sp.dma_start(us[SH * s:SH * s + SH, :, :], uv[s]).then_inc(S("us_loaded"), 16)
            load(IT["w_out"][0])
            sp.wait_ge(S("dec_ready"), 1)
            sp.wait_ge(S("s5V_re"), 2)
            sp.wait_ge(S("s5V_im"), 2)
            load(IT["w_out"][1])
            sp.wait_ge(S("y_done"), 4)
            for i in range(2):
                m0 = moe_item[i]
                for e in range(GE):
                    load(m0 + e)
                wviews = [I["moe_w_gate"][i].rearrange("g j (p k) n -> p (g j) (k n)", k=KD),
                          I["moe_w_up"][i].rearrange("g j (p k) n -> p (g j) (k n)", k=KD),
                          I["moe_w_down"][i].rearrange("g j (p k) n -> p (g j) (k n)", k=2)]
                with sp.Fori(1, NSTEP) as g:
                    for j in range(GE):
                        s = items[m0 + j][0]
                        sp.wait_ge(S("d_done"), g * GE + (NE * i + j - GE + 1))
                        for c, w in enumerate(wviews):
                            sp.dma_start(ring[s][:, 2048 * c:2048 * c + 2048],
                                         w[:, bass.ds(g * GE + j, 1), :].rearrange("p e n -> p (e n)"))\
                                .then_inc(loaded[s], 16)
                def more(n):
                    sp.wait_ge(S(f"ov_free{i}"), n + 1)
                    e = n % NE
                    for c, w in enumerate(wviews):
                        sp.dma_start(ring[s_ov][:, 2048 * c:2048 * c + 2048],
                                     w[:, bass.ds(e, 1), :].rearrange("p e n -> p (e n)"))\
                            .then_inc(S(f"ov_loaded{i}"), 16)

                s_ov = items[m0][0]
                sp.wait_ge(S("d_done"), NE * (i + 1))
                overflow(sp, i, more, lambda: sp.sem_inc(S(f"ov_free{i}"), 1),
                         lambda: sp.wait_ge(S(f"ov_free{i}"), NOV + 1))
                for n in IT["ple"][i]:
                    load(n)
                if i == 0:
                    for n in IT["qkv"] + IT["wo"]:
                        load(n)
            for n in range(4):
                c, t = divmod(n, 2)
                cs = slice(512 * c, 512 * c + 512)
                sp.wait_ge(S("ple_used"), 4 + n + 1)
                sp.dma_start(out[0, P * t:P * t + P, cs], x[:, t, cs]).then_inc(S("stored"), 16)
            sp.wait_ge(S("stored"), 64)

        @block.gpsimd
        def _(pool):
            link = seq(pool, S("pool_own"))
            pool.memset(ident[:, :], 0.0)
            pool.memset(mask[:, :, :], 1.0)
            pool.memset(tri[:, :], 1.0)
            pool.memset(ones[:, :], 1.0)
            link(pool.memset(negh[:, :], 0.0))
            pool.affine_select(out=ident[:, :], in_=ident[:, :], compare_op=ALU.not_equal, fill=1.0, base=0,
                               pattern=[[-1, P]], channel_multiplier=1).then_inc(S("ident_ready"), 1)
            pool.affine_select(out=tri[:, :], in_=tri[:, :], compare_op=ALU.is_gt, fill=0.0, base=0,
                               pattern=[[1, P]], channel_multiplier=-1)
            pool.affine_select(out=mask[:, 0, :], in_=mask[:, 0, :], compare_op=ALU.is_ge, fill=0.0,
                               base=SH - 1, pattern=[[SH, L], [0, SH]], channel_multiplier=-1)
            link(pool.affine_select(out=mask[:, 1, :], in_=mask[:, 1, :], compare_op=ALU.is_ge, fill=0.0,
                                    base=0, pattern=[[-SH, L], [0, SH]], channel_multiplier=1))
            link(pool.iota(wp_i[0:64, :], pattern=[[-1, L]], base=L - 1, channel_multiplier=0))
            link(pool.iota(wp_i[64:P, :], pattern=[[1, L]], base=0, channel_multiplier=0))
            link(pool.iota(cidx_i[0:64, :], pattern=[[1, NC_]], base=0, channel_multiplier=0))
            link(pool.iota(cidx_i[64:P, :], pattern=[[-1, NC_]], base=NC_ - 1, channel_multiplier=0))
            link(pool.iota(iota_i[:, :], pattern=[[1, GS]], base=0, channel_multiplier=0))
            pool.tensor_copy(wp[:, :], wp_i[:, :])
            pool.tensor_copy(cidx[:, :], cidx_i[:, :])
            pool.tensor_copy(iota_slot[:, :], iota_i[:, :])
            pool.tensor_copy(iota_e[:, :], iota_i[:, 0:NE])
            for b in (0, 64):
                link(pool.affine_select(out=negh[b:b + 64, 0:GW - WC], in_=negh[b:b + 64, 0:GW - WC],
                                        compare_op=ALU.is_ge, fill=MASKV, base=WC // 2,
                                        pattern=[[1, GW - WC]], channel_multiplier=-1))
                link(pool.affine_select(out=negh[b:b + 64, WC:GW], in_=negh[b:b + 64, WC:GW],
                                        compare_op=ALU.is_ge, fill=MASKV, base=WC // 2 - 1 - WC,
                                        pattern=[[-1, GW - WC]], channel_multiplier=1))
            pool.memset(mhalf[:, :], -0.5).then_inc(S("consts"), 1)

            def norm_pow(n):
                pool.wait_ge(S("ms_ready"), n + 1)
                pool.tensor_tensor(rstd[:, 0:TT], ms[:, 0:TT], mhalf[:, 0:TT], ALU.pow).then_inc(S("rstd_ready"), 1)

            pool.dma_start(rp[:, :, :], I["nat_rpb"][0].rearrange("a b c -> (a b) c")
                           .rearrange("(p a) c -> p a c", a=2))\
                .then_inc(S("rp_loaded"), 16)
            pool.wait_ge(S("rp_loaded"), 16)
            link(pool.tensor_copy(rpf[:, :, :], rp[:, :, ::-1]))
            pool.dma_start(rpbr.rearrange("(p a) c -> p a c", a=2), rpf[:, :, :]).then_inc(S("rpbr_written"), 16)

            norm_pow(0)
            pool.wait_ge(S("pw_ready"), 1)
            g0 = slice(16, 32)
            link(pool.tensor_tensor(s5W[:, 1, g0], bc(bbar[:, 0, g0], 2, L), bc(pw[:, 1, g0], 3, SH), ALU.mult))
            link(pool.tensor_tensor(tmpP[:, :, :, :], bc(bbar[:, 1, g0], 2, L), bc(pw[:, 0, g0], 3, SH), ALU.mult))
            pool.tensor_tensor(s5W[:, 1, g0], s5W[:, 1, g0], tmpP[:, :, :, :], ALU.add).then_inc(S("s5W_im1"), 1)
            pool.wait_ge(S("s5W_im1"), 1)
            pool.wait_ge(S("cT_ready"), 2)
            for q in range(2):
                g0 = slice(16 * q, 16 * q + 16)
                link(pool.tensor_tensor(s5V[:, 0, g0], bc(cT[:, 0, g0], 2, L), bc(pw[:, 2, g0], 3, SH), ALU.mult))
                link(pool.tensor_tensor(tmpP[:, :, :, :], bc(cT[:, 1, g0], 2, L), bc(pw[:, 7, g0], 3, SH), ALU.mult))
                pool.tensor_tensor(s5V[:, 0, g0], s5V[:, 0, g0], tmpP[:, :, :, :], ALU.add)\
                    .then_inc(S("s5V_re"), 1)
                pool.wait_ge(S("s5V_re"), q + 1)
            pool.wait_ge(S("rpbr_written"), 16)
            norm_pow(1)
            norm_pow(2)
            norm_pow(3)
            for part in range(2):
                if part == 0:
                    pool.wait_ge(S("x_ready"), 3)
                else:
                    pool.wait_ge(S("k_T"), 2 * TT)
                hp = NH // 2
                for rq in range(ROWS):
                    for rk in range(ROWS):
                        off = part * hp * (2 * WR - 1) * (2 * WC - 1) + (rk - rq + WR - 1) * (2 * WC - 1) + WC - GW
                        src = bass.AP(rpbr.tensor, off,
                                      [[1, GW], [(2 * WR - 1) * (2 * WC - 1), hp], [1, GW]])
                        p0 = 64 * (rq % 2)
                        pool.dma_start(bias[part][p0:p0 + 64, :, rq // 2, rk, :], src)\
                            .then_inc(S(f"bias_loaded{part}"), 16)
                pool.wait_ge(S(f"bias_loaded{part}"), 16 * ROWS * ROWS)
                for hh in range(hp):
                    b = bias[part][:, hh].rearrange("p a r c -> p (a r) c")
                    pool.tensor_tensor(b, b, bc(negh[:, ::-1], 1, TT * ROWS), ALU.add).then_inc(S("bias_ready"), 1)
                if part == 0:
                    for t in range(TT):
                        pool.wait_ge(S("qms_ready"), t + 1)
                        pool.tensor_tensor(qrs[:, t, :], qms[:, t, :], mhalf[:, :], ALU.pow)\
                            .then_inc(S("qrs_ready"), 1)
            norm_pow(4)
            norm_pow(5)

        @block.scalar
        def _(ac):
            link = seq(ac, S("act_own"))
            def load_gain(n):
                dst, sem, _ = gain_of(n)
                ac.dma_start(dst[:, :], bc(gains[n], 0, P)).then_inc(sem, 16)

            def load_router(i):
                ac.dma_start(wr[:, :, 0:NG], kp(I["moe_w_group"][i], KD)).then_inc(S("router_loaded"), 16)
                ac.dma_start(wr[:, :, NG:], kp(I["moe_w_expert"][i], KD)).then_inc(S("router_loaded"), 16)
                ac.dma_start(rbias[:, 0:NG], bc(I["moe_b_group"][i], 0, P)).then_inc(S("router_loaded"), 16)
                ac.dma_start(rbias[:, NG:], bc(I["moe_b_expert"][i], 0, P)).then_inc(S("router_loaded"), 16)

            ac.dma_start(lam[:, 0], I["s5_lam_re"][0].rearrange("d g p -> g d p")).then_inc(S("lam_loaded"), 16)
            ac.dma_start(lam[:, 1], I["s5_lam_im"][0].rearrange("d g p -> g d p")).then_inc(S("lam_loaded"), 16)
            ac.dma_start(ldt[:, :], I["s5_log_dt"][0].rearrange("d g -> g d"),
                         allow_slow_non_contiguous=True).then_inc(S("lam_loaded"), 16)
            for c, nm in enumerate(("s5_c_re", "s5_c_im")):
                for d in range(2):
                    ac.dma_start(craw[:, c, :, d, :], I[nm][0, d].rearrange("(a b) h p -> (b h) a p", b=8))\
                        .then_inc(S("c_loaded"), 16)
            for c, nm in enumerate(("s5_b_re", "s5_b_im")):
                for d in range(2):
                    ac.dma_start(braw[64 * d:64 * d + 64, c], I[nm][0, d].rearrange("g p h -> p g h"))\
                        .then_inc(S("b_loaded"), 16)
            load_gain(0)
            ac.dma_start(dskip[:, :], I["s5_d"][0].rearrange("(k p) -> p k", p=P),
                         allow_slow_non_contiguous=True).then_inc(S("d_loaded"), 16)

            def norm_sq(n):
                if n == 0:
                    ac.wait_ge(S("x_loaded"), 16)
                else:
                    ac.wait_ge(S("x_ready"), n)
                for t in range(TT):
                    ac.activation(h[:, t, :], x[:, t, :], ACT.Square, accum_out=ss[:, t:t + 1])\
                        .then_inc(S("ss_ready"), 1)

            def split_evict(n):
                for t, sem in enumerate(("h_T", "h_T2")):
                    for kq in range(2):
                        ac.wait_ge(S(sem), 2 * n + kq + 1)
                        ac.activation(hTh[:, 4 * kq:4 * kq + 4, P * t:P * t + P],
                                      PS[:, NB + 2 * t + kq, :].rearrange("p (k t) -> p k t", k=4),
                                      ACT.Copy).then_inc(S("hTh_ready"), 1)

            def dense_hi(n):
                q = 4 * dense.index(n)
                arrived(ac, n)
                for c in range(4):
                    if q + c >= 4:
                        ac.wait_ge(S("split_done"), q + c - 3)
                    ac.activation(dwh[:, c], dense_w(n, c)[0], ACT.Copy).then_inc(S("dense_hi"), 1)

            def norm_evict(n, dst):
                for kq in range(2):
                    ac.wait_ge(S("h_T"), 2 * n + kq + 1)
                    ac.activation(dst[:, 4 * kq:4 * kq + 4, 0:P], PS[:, NB + kq, :].rearrange("p (k t) -> p k t", k=4),
                                  ACT.Copy).then_inc(S("hT_a"), 1)

            ac.wait_ge(S("lam_loaded"), 48)
            ac.activation(dtt[:, :], ldt[:, :], ACT.Exp).then_inc(S("dt_ready"), 1)
            ac.wait_ge(S("ang_ready"), 1)
            ac.activation(pq[:, 5], pq[:, 0], ACT.Exp).then_inc(S("trig_ready"), 1)
            ac.activation(pq[:, 6], pq[:, 3], ACT.Sin).then_inc(S("trig_ready"), 1)
            ac.activation(pq[:, 7], pq[:, 4], ACT.Sin).then_inc(S("trig_ready"), 1)
            for c in range(2):
                ac.wait_ge(S("c_T"), c + 1)
                ac.activation(cT[:, c], PS[:, 1 + c, :].rearrange("p (g h) -> p g h", h=SH), ACT.Copy)\
                    .then_inc(S("cT_ready"), 1)
            ac.wait_ge(S("phase_ready"), 1)
            ac.activation(pw[:, 3], pw[:, 0], ACT.Exp)
            ac.activation(pw[:, 4], pw[:, 0], ACT.Exp, scale=-1.0)
            ac.activation(t32[:, 1], prmT[:, 0], ACT.Exp, scale=float(L))
            ac.activation(pw[:, 5], pw[:, 1], ACT.Sin, scale=TURN)
            ac.activation(pw[:, 6], pw[:, 2], ACT.Sin, scale=TURN).then_inc(S("powx_ready"), 1)
            norm_sq(0)
            norm_evict(0, s5hT)
            ac.wait_ge(S("rpbr_written"), 16)
            load_router(0)
            ac.wait_ge(S("u_done"), 1)
            for b in range(2):
                ac.activation(uT[:, 2 * b:2 * b + 2].rearrange("p k s c -> p k s c"),
                              PS[:, 4 + b, :].rearrange("p (k c s) -> p k s c", k=2, s=L), ACT.Copy)\
                    .then_inc(S("uT_half"), 1)
            for n in range(SG // 2):
                ac.wait_ge(S("W_T"), n + 1)
                ac.activation(s5WT[:, :, 2 * n:2 * n + 2, :].rearrange("p r g n -> p g r n"),
                              PS[:, 2 + n % 2, :].rearrange("p (g r n) -> p g r n", g=2, r=2), ACT.Copy)\
                    .then_inc(S("WT_ready"), 1)
            ac.wait_ge(S("cphase_ready"), 1)
            ac.activation(stab[:, :, :], ct0[:, :, :], ACT.Sin, scale=TURN)
            ac.activation(ctab[:, :, :], ct1[:, :, :], ACT.Sin, scale=TURN).then_inc(S("ctab_ready"), 1)

            def y_evict(k):
                ac.wait_ge(S("y_done"), k + 1)
                if k >= 2:
                    ac.wait_ge(S("y_T"), k - 1)
                b = 2 * (k % 2)
                ac.activation(ys[k % 2][:, :, :, :].rearrange("c s g h -> c g s h"),
                              PS[0:NC_, b:b + 2, :].rearrange("c b (g s h) -> c (b g) s h", g=4, s=L),
                              ACT.Copy).then_inc(S("ys_part"), 1)

            def gelu_tanh(k):
                ac.wait_ge(S("inner_ready"), k + 1)
                ac.activation(yT[3][:, k, :], yT[2][:, k, :], ACT.Tanh, scale=math.sqrt(2 / math.pi))\
                    .then_inc(S("tanh_ready"), 1)

            y_evict(0)
            y_evict(1)
            y_evict(2)
            gelu_tanh(0)
            y_evict(3)
            load_gain(1)
            gelu_tanh(1)
            gelu_tanh(2)
            gelu_tanh(3)
            for n in range(4):
                ac.wait_ge(S("glu_done"), n + 1)
                if n >= 2:
                    ac.wait_ge(S("glu_used"), n - 1)
                ac.activation(glu[n % 2][:, :], PS[:, 5 + 2 * (n % 2), :], ACT.Sigmoid).then_inc(S("sig_ready"), 1)

            def evict(m, dst, src):
                ac.wait_ge(S("m_written"), m + 1)
                ac.activation(dst, src, ACT.Copy).then_inc(S("m_evicted"), 1)

            def chunk(i, g, jj, c):
                n = 4 * NE * i + 4 * GE * g + 4 * jj + c
                s = items[moe_item[i] + jj % GE][0]
                if c == 0:
                    ac.wait_ge(loaded[s], expert_loaded(i, g, jj))
                if not (isinstance(n, int) and n < 4):
                    ac.wait_ge(S("split_used"), n - 3)
                r = ring[s][:, 0:4096].rearrange("p (u n) -> p u n", u=2)[:, :, 512 * c:512 * c + 512]
                ac.activation(whi[:, c].rearrange("p k (u f) -> p u k f", u=2),
                              r.rearrange("p u (k f) -> p u k f", k=2), ACT.Copy).then_inc(S("hi_ready"), 1)

            def fold(i, e):
                ac.wait_ge(S("split_used"), (NE * i + e) * 4 + 4)
                ac.activation(gu[:, :], PS[64:P, 0, :], ACT.Copy).then_inc(S("flo_ready"), 1)

            def silu(i, e):
                ac.wait_ge(S("gu_ready"), NE * i + e + 1)
                ac.activation(act[:, :], gu[:, 0:FF], ACT.Silu).then_inc(S("silu_ready"), 1)

            def units(par, lst, m):
                for n, u in enumerate(lst):
                    b = FIRST_BANKS[n % len(FIRST_BANKS)] if lst is ALL_UNITS else 1
                    if u == "selT":
                        evict(m + n, selT[:, par].rearrange("p a t -> p (a t)"), PS[:, b, :])
                    elif u == "weights":
                        evict(m + n, wslot[0:64, par, :], PS[0:64, b, 0:GE])
                    else:
                        evict(m + n, xg[:, par, :, u].rearrange("p e c j -> p c e j"),
                              PS[:, b, :].rearrange("p (c e j) -> p c e j", c=2, e=GE))

            def step(i, g, par, j, last):
                e = g * GE + j
                off = j if last else M_POS[j][0]
                b = j % 2
                evict(use(i, g, off), actT[:, b, :, CAP * b:CAP * b + CAP],
                      PS[:, 1, 0:2 * CAP].rearrange("p (k t) -> p k t", k=2))
                more = not (last and j >= 2)
                nxt = not (last and j == 3)

                def part(n):
                    if not last:
                        units(1 - par, UNITS[j][n], use(i, g, M_POS[j][n + 1]))

                if more:
                    chunk(i, g, j + 2, 0)
                part(0)
                if more:
                    chunk(i, g, j + 2, 1)
                if nxt:
                    fold(i, e + 1)
                if last and j == 2:
                    load_gain(2 + 3 * i)
                part(1)
                if more:
                    chunk(i, g, j + 2, 2)
                if nxt:
                    silu(i, e + 1)
                part(2)
                if more:
                    chunk(i, g, j + 2, 3)
                if j % 2:
                    pair = g * 2 + j // 2 + NE // 2 * i
                    ac.wait_ge(S("d_done"), NE * i + e + 1)
                    if not (isinstance(pair, int) and pair == 0):
                        ac.wait_ge(S("comb_done"), pair)
                    for n in range(2):
                        ac.activation(ohi[:, 512 * n:512 * n + 512], PS[:, 2 + n, :], ACT.Copy)\
                            .then_inc(S("ohi_ready"), 1)

            def moe(i):
                norm_sq(1 + 3 * i)
                norm_evict(1 + 3 * i, hT)
                for c in range(2):
                    chunk(i, 0, 0, c)
                ac.wait_ge(S("top_ready"), i + 1)
                for t in range(TT):
                    ac.activation(gex[:, t, :], gl[:, t, 0:NG], ACT.Exp, bias=ngm[:, t:t + 1],
                                  accum_out=gsum[:, t:t + 1])
                ac.activation(e21[:, :], dlt[:, :], ACT.Exp).then_inc(S("gex_ready"), 1)
                for c in range(2, 4):
                    chunk(i, 0, 0, c)
                units(0, ALL_UNITS, M_BASE * i)
                chunk(i, 0, 1, 0)
                chunk(i, 0, 1, 1)
                fold(i, 0)
                chunk(i, 0, 1, 2)
                silu(i, 0)
                chunk(i, 0, 1, 3)
                for j in range(GE):
                    step(i, 0, 0, j, False)
                with ac.Fori(0, (NSTEP - 2) // 2) as r:
                    for sub in (1, 2):
                        for j in range(GE):
                            step(i, r * 2 + sub, sub % 2, j, False)
                for j in range(GE):
                    step(i, NSTEP - 1, 1, j, True)
                moe_more(i)

            def moe_more(i):
                def more(n):
                    name = lambda what: S(f"ov_{what}{i}")
                    ac.wait_ge(name("gu"), n + 1)
                    ac.activation(slu[:, :], PS[0:CAP, 2, 0:FF], ACT.Silu).then_inc(name("silu"), 1)

                overflow(ac, i, more)

            def ple(i):
                ac.wait_ge(S("p_T"), i + 1)
                ac.activation(pT[:, :, :].rearrange("p k t -> p (k t)"), PS[:, 0, :], ACT.Copy).then_inc(S("pT_ready"), 1)
                dense_hi(IT["ple"][i][0])
                norm_sq(2 + 3 * i)
                if i == 0:
                    load_gain(3)
                split_evict(2 + 3 * i)
                dense_hi(IT["ple"][i][2])
                for n in range(4):
                    k = 4 * i + n
                    ac.wait_ge(S("split_done"), 4 * dense.index(IT["ple"][i][2 * (n // 2)]) + 4)
                    if k >= 2:
                        ac.wait_ge(S("ple_used"), k - 1)
                    ac.activation(sg[n % 2][:, :], PS[:, 4 + n, :], ACT.Sigmoid).then_inc(S("sg_ready"), 1)

            moe(0)
            ple(0)

            norm_sq(3)
            for c, nm in enumerate(("nat_q_norm", "nat_k_norm")):
                for d in range(2):
                    ac.dma_start(qkw[64 * d:64 * d + 64, c:c + 1], I[nm][0].rearrange("(p a) -> p a", a=1))\
                        .then_inc(S("qkw_loaded"), 16)
            split_evict(3)
            ac.wait_ge(S("h_ready"), TT * 4)
            load_gain(4)
            load_router(1)
            for w in range(7):
                if w < 6:
                    dense_hi(IT["qkv"][w])
                if w:
                    v_ = w - 1
                    ac.wait_ge(S("split_done"), 4 * dense.index(IT["qkv"][v_]) + 4)
                    dst = qk[:, 0, 8 * v_:8 * v_ + 8, :].rearrange("p a d -> p (a d)") if v_ < 4 else \
                        vt[:, 0, 512 * (v_ - 4):512 * (v_ - 4) + 512]
                    ac.activation(dst, PS[:, 2 * (v_ % 2), :], ACT.Copy).then_inc(S("qkv_a"), 1)
                if w == 5:
                    for t in range(TT):
                        ac.wait_ge(S("qkv_d"), 4)
                        ac.wait_ge(S("qkv_a"), 4)
                        if t:
                            ac.wait_ge(S("qss_ready"), t)
                        ac.activation(sq[:, :, :], qk[:, t], ACT.Square).then_inc(S("sq_ready"), 1)
            ac.wait_ge(S("qkw_loaded"), 64)
            link(ac.activation(qkw8[:, :], qkw[:, 0:1], ACT.Copy, scale=1 / math.sqrt(HD)))
            for t in range(TT):
                for n in range(2):
                    ac.wait_ge(S("q_T"), 2 * t + n + 1)
                    ac.activation(qT[:, 4 * n:4 * n + 4, P * t:P * t + P],
                                  PS[:, 4 + n, :].rearrange("p (a t) -> p a t", a=4), ACT.Copy,
                                  scale=qkw8[:, 0:1]).then_inc(S("qT_ready"), 1)
            for a in range(NH + 2):
                if a < NH:
                    ac.wait_ge(S("mx_ready"), a + 1)
                    for t in range(TT):
                        ac.activation(prob[:, a % 4, t, :], prob[:, a % 4, t, :], ACT.Exp, bias=mx[:, a % 4, t:t + 1],
                                      accum_out=rs[:, a % 4, t:t + 1]).then_inc(S("exp_ready"), 1)
                if a >= 2:
                    b = a - 2
                    ac.wait_ge(S("prob_T"), b + 1)
                    if b >= 2:
                        ac.wait_ge(S("pv_done"), b - 1)
                    ac.activation(probT[:, b % 2].rearrange("p a t -> p (a t)"), PS[:, 2 + b % 2, :], ACT.Copy)\
                        .then_inc(S("probT_ready"), 1)
            moe(1)
            ple(1)

        @block.vector
        def _(ve):
            link = seq(ve, S("dve_own"))
            tt = ve.tensor_tensor
            ts = ve.tensor_scalar
            stt = ve.scalar_tensor_tensor

            def norm_scale(n):
                ve.wait_ge(S("ss_ready"), TT * (n + 1))
                ts(ms[:, 0:TT], ss[:, 0:TT], 1.0 / D, EPS, ALU.mult, ALU.add).then_inc(S("ms_ready"), 1)
                gain, sem, value = gain_of(n)
                ve.wait_ge(sem, value)
                ve.wait_ge(S("rstd_ready"), n + 1)
                for t in range(TT):
                    stt(h[:, t, :], x[:, t, :], rstd[:, t:t + 1], gain[:, :], ALU.mult, ALU.mult)\
                        .then_inc(S("h_ready"), 1)

            def split_evict(n):
                for t in range(TT):
                    for kq in range(2):
                        ve.wait_ge(S("hTh_ready"), 4 * SPLIT[n] + 2 * t + kq + 1)
                        r = hTh[:, 4 * kq:4 * kq + 4, P * t:P * t + P]
                        tt(hTl[:, 4 * kq:4 * kq + 4, P * t:P * t + P],
                           PS[:, NB + 2 * t + kq, :].rearrange("p (k t) -> p k t", k=4), r.bitcast(F32),
                           ALU.subtract).then_inc(S("hTl_ready"), 1)

            def dense_lo(n, c0, c1):
                for c in range(c0, c1):
                    ve.wait_ge(S("dense_hi"), 4 * dense.index(n) + c + 1)
                    w, lo = dense_w(n, c)
                    tt(lo, w, dwh[:, c].bitcast(F32), ALU.subtract).then_inc(S("dense_lo"), 1)

            def norm_evict(n, dst):
                for kq in range(2):
                    ve.wait_ge(S("h_T2"), 2 * n + kq + 1)
                    ve.tensor_copy(dst[:, 4 * kq:4 * kq + 4, P:T],
                                   PS[:, NB + 2 + kq, :].rearrange("p (k t) -> p k t", k=4)).then_inc(S("hT_d"), 1)

            ve.wait_ge(S("lam_loaded"), 48)
            ve.wait_ge(S("dt_ready"), 1)
            v = [pq[:, n].rearrange("g (d p) -> g d p", d=2) for n in range(14)]
            for d in range(2):
                ts(v[0][:, d], lam[:, 0, d, :], dtt[:, d:d + 1], None, ALU.mult)
                link(ts(v[1][:, d], lam[:, 1, d, :], dtt[:, d:d + 1], None, ALU.mult))
            link(ts(v[2], v[1], 1 / (2 * math.pi), MAGIC, ALU.mult, ALU.add))
            link(ts(v[2], v[2], MAGIC, None, ALU.subtract))
            link(stt(v[3], v[2], -TWO_PI_HI, v[1], ALU.mult, ALU.add))
            link(stt(v[3], v[2], -TWO_PI_LO, v[3], ALU.mult, ALU.add))
            link(ts(v[3], v[3], TURN / 2, -TURN / 2, ALU.min, ALU.max))
            link(stt(v[4], v[3], -1.0, v[3], ALU.mult, ALU.min))
            ts(v[4], v[4], math.pi / 2, None, ALU.add).then_inc(S("ang_ready"), 1)
            re, im = lam[:, 0], lam[:, 1]
            link(tt(v[10], re, re, ALU.mult))
            link(tt(v[11], im, im, ALU.mult))
            link(tt(v[10], v[10], v[11], ALU.add))
            link(ve.reciprocal(v[10], v[10]))
            ve.wait_ge(S("trig_ready"), 3)
            link(tt(v[8], v[5], v[7], ALU.mult))
            link(tt(v[9], v[5], v[6], ALU.mult))
            link(ts(v[8], v[8], -1.0, None, ALU.add))
            link(tt(v[11], v[8], re, ALU.mult))
            link(tt(v[12], v[9], im, ALU.mult))
            link(tt(v[11], v[11], v[12], ALU.add))
            link(tt(v[12], v[9], re, ALU.mult))
            link(tt(v[13], v[8], im, ALU.mult))
            link(tt(v[12], v[12], v[13], ALU.subtract))
            link(tt(v[11], v[11], v[10], ALU.mult))
            link(tt(v[12], v[12], v[10], ALU.mult))
            ts(v[2], v[3], 1 / (2 * math.pi), None, ALU.mult).then_inc(S("coef_ready"), 1)
            ve.wait_ge(S("prm_T"), 1)
            link(ve.tensor_copy(prmT[:, :, :].rearrange("p a g -> p (a g)"), PS[:, 0, 0:4 * SG]))
            ve.wait_ge(S("consts"), 1)
            link(tt(pw[:, 0], bc(prmT[:, 0, :], 2, L), bc(wp[:, :], 1, SG), ALU.mult))
            link(tt(pw[:, 1], bc(prmT[:, 1, :], 2, L), bc(wp[:, :], 1, SG), ALU.mult))

            def turns(ph, quarter):
                link(ts(quarter, ph, MAGIC, None, ALU.add))
                link(ts(quarter, quarter, MAGIC, None, ALU.subtract))
                link(tt(ph, ph, quarter, ALU.subtract))
                link(stt(quarter, ph, -1.0, ph, ALU.mult, ALU.min))
                return ts(quarter, quarter, 0.25, None, ALU.add)

            turns(pw[:, 1], pw[:, 2]).then_inc(S("phase_ready"), 1)
            ve.wait_ge(S("b_loaded"), 64)
            cr, ci = bc(prmT[:, 2, :], 2, SH), bc(prmT[:, 3, :], 2, SH)
            tmp = tmpD[:, 0:4].rearrange("p g l h -> p (g l) h")
            link(tt(bbar[:, 0], braw[:, 0], cr, ALU.mult))
            link(tt(tmp, braw[:, 1], ci, ALU.mult))
            link(tt(bbar[:, 0], bbar[:, 0], tmp, ALU.subtract))
            link(tt(bbar[:, 1], braw[:, 1], cr, ALU.mult))
            link(tt(tmp, braw[:, 0], ci, ALU.mult))
            link(tt(bbar[:, 1], bbar[:, 1], tmp, ALU.add))
            ve.wait_ge(S("powx_ready"), 1)
            link(tt(pw[:, 0], pw[:, 3], pw[:, 6], ALU.mult))
            link(tt(pw[:, 1], pw[:, 3], pw[:, 5], ALU.mult))
            link(tt(pw[:, 2], pw[:, 4], pw[:, 6], ALU.mult))
            tt(pw[:, 7], pw[:, 4], pw[:, 5], ALU.mult).then_inc(S("pw_ready"), 1)
            norm_scale(0)
            norm_evict(0, s5hT)
            ve.wait_ge(S("pw_ready"), 1)
            td = tmpD[:, :, :, :]
            for q in range(2):
                gg = slice(16 * q, 16 * q + 16)
                br, bi = bc(bbar[:, 0, gg], 2, L), bc(bbar[:, 1, gg], 2, L)
                pr_, pi = bc(pw[:, 0, gg], 3, SH), bc(pw[:, 1, gg], 3, SH)
                link(tt(s5W[:, 0, gg], br, pr_, ALU.mult))
                link(tt(td, bi, pi, ALU.mult))
                tt(s5W[:, 0, gg], s5W[:, 0, gg], td, ALU.subtract).then_inc(S("s5W_re"), 1)
                ve.wait_ge(S("s5W_re"), q + 1)
                if q == 0:
                    link(tt(s5W[:, 1, gg], br, pi, ALU.mult))
                    link(tt(td, bi, pr_, ALU.mult))
                    tt(s5W[:, 1, gg], s5W[:, 1, gg], td, ALU.add).then_inc(S("s5W_im0"), 1)
                    ve.wait_ge(S("s5W_im0"), 1)
            t8, t8n = t32[:, 2], t32[:, 3]
            link(ts(t8, prmT[:, 1, :], float(L), None, ALU.mult))
            link(ts(t8n, t8, MAGIC, None, ALU.add))
            link(ts(t8n, t8n, MAGIC, None, ALU.subtract))
            link(tt(t8, t8, t8n, ALU.subtract))
            link(tt(ct0[:, :, :], bc(t8, 2, NC_), bc(cidx[:, :], 1, SG), ALU.mult))
            turns(ct0[:, :, :], ct1[:, :, :]).then_inc(S("cphase_ready"), 1)
            ve.wait_ge(S("cT_ready"), 2)
            for q in range(2):
                gg = slice(16 * q, 16 * q + 16)
                link(tt(s5V[:, 1, gg], bc(cT[:, 0, gg], 2, L), bc(pw[:, 7, gg], 3, SH), ALU.mult))
                link(tt(td, bc(cT[:, 1, gg], 2, L), bc(pw[:, 2, gg], 3, SH), ALU.mult))
                tt(s5V[:, 1, gg], s5V[:, 1, gg], td, ALU.subtract).then_inc(S("s5V_im"), 1)
                ve.wait_ge(S("s5V_im"), q + 1)
            ve.wait_ge(S("s5V_re"), 2)
            link(ve.tensor_copy(dec[:, :, :], bc(t32[:, 1], 2, NC_)))
            ve.memset(dec[0:64, :, NC_ - 1:NC_], 0.0)
            ve.memset(dec[64:P, :, 0:1], 0.0).then_inc(S("dec_ready"), 1)
            ve.wait_ge(S("dec_ready"), 1)

            def mask_T(n):
                ve.wait_ge(S("T_done"), 2 * n + 2)
                for d in range(2):
                    dn = tt(tmsk[:, d], PS[:, 2 * (n % 2) + d, :].rearrange("p (g n) -> p g n", g=4),
                            bc(mask[:, d, :], 1, 4), ALU.mult)
                link(dn)
                tt(s5T[:, 4 * n:4 * n + 4, :], tmsk[:, 0], tmsk[:, 1], ALU.add).then_inc(S("s5T_ready"), 1)
                ve.wait_ge(S("s5T_ready"), n + 1)

            ve.wait_ge(S("ctab_ready"), 1)
            ve.wait_ge(S("v_done"), 1)
            vr = PS[:, 4:6, :].rearrange("p b (g c) -> p (b g) c", c=NC_)
            vi = PS[:, 6:8, :].rearrange("p b (g c) -> p (b g) c", c=NC_)
            C_, S_ = ctab[:, :, :], stab[:, :, :]
            mr, mi, qr, qi, ta, tb = [sc[n][:, :, :] for n in range(6)]
            sr, si = mr, mi
            link(tt(mr, vr, C_, ALU.mult))
            link(tt(ta, vi, S_, ALU.mult))
            link(tt(mi, vi, C_, ALU.mult))
            link(tt(tb, vr, S_, ALU.mult))
            link(tt(mr, mr, ta, ALU.add))
            link(tt(mi, mi, tb, ALU.subtract))
            mask_T(0)
            N = SG * NC_
            fl = [sc[n][:, :, :].rearrange("p g c -> p (g c)") for n in range(4)]
            df = dec[:, :, :].rearrange("p g c -> p (g c)")
            for q in (2, 3):
                ve.memset(fl[q][0:64, 0:1], 0.0)
                link(ve.memset(fl[q][64:P, N - 1:N], 0.0))
            for m, q in ((0, 2), (1, 3)):
                link(ve.tensor_tensor_scan(fl[q][0:64, 1:N], fl[m][0:64, 0:N - 1], df[0:64, 0:N - 1], 0.0,
                                           ALU.add, ALU.mult))
                link(ve.tensor_tensor_scan(fl[q][64:P, N - 2::-1], fl[m][64:P, N - 1:0:-1], df[64:P, N - 1:0:-1],
                                           0.0, ALU.add, ALU.mult))
                mask_T(1 + m)
            link(tt(sr, qr, C_, ALU.mult))
            link(tt(ta, qi, S_, ALU.mult))
            link(tt(si, qr, S_, ALU.mult))
            link(tt(tb, qi, C_, ALU.mult))
            tt(sr, sr, ta, ALU.subtract).then_inc(S("S_ready"), 1)
            tt(si, si, tb, ALU.add).then_inc(S("S_ready"), 1)
            for n in range(3, SG // 4):
                mask_T(n)
            ve.wait_ge(S("d_loaded"), 16)
            uf = uT[:, :, :, :].rearrange("p k s c -> p k (s c)")

            def gelu_inner(k):
                y1, y2 = yT[1][:, k, :], yT[2][:, k, :]
                ve.wait_ge(S("y_T"), k + 1)
                link(stt(y1, uf[:, k, :], dskip[:, k:k + 1], PS[:, 4 + k, 0:T], ALU.mult, ALU.add))
                link(tt(y2, y1, y1, ALU.mult))
                link(ts(y2, y2, 0.044715, 1.0, ALU.mult, ALU.add))
                tt(y2, y2, y1, ALU.mult).then_inc(S("inner_ready"), 1)

            def gelu_outer(k):
                y1, y3, y4 = [yT[n][:, k, :] for n in (1, 3, 4)]
                ve.wait_ge(S("tanh_ready"), k + 1)
                link(ts(y3, y3, 0.5, 0.5, ALU.mult, ALU.add))
                tt(y4.rearrange("p (c s) -> p s c", s=L), y3.rearrange("p (s c) -> p s c", s=L),
                   y1.rearrange("p (s c) -> p s c", s=L), ALU.mult).then_inc(S("gelu_ready"), 1)

            for k in range(4):
                gelu_inner(k)
                if k:
                    gelu_outer(k - 1)
            gelu_outer(3)
            for n in range(4):
                t, c = divmod(n, 2)
                ve.wait_ge(S("sig_ready"), n + 1)
                link(tt(glu[n % 2][:, :], PS[:, 4 + 2 * (n % 2), :], glu[n % 2][:, :], ALU.mult))
                xs = x[:, t, 512 * c:512 * c + 512]
                ins = tt(xs, xs, glu[n % 2][:, :], ALU.add)
                ins.then_inc(S("glu_used"), 1)
                ve.wait_ge(S("glu_used"), n + 1)
            ve.sem_inc(S("x_ready"), 1)

            def route(i):
                ve.memset(gl[:, :, :], 3 * MASKV)
                ve.wait_ge(S("router_loaded"), 64 * (i + 1))
                ve.wait_ge(S("logits_done"), i + 1)
                lp = PS[:, 0, 0:TT * (NG + NE)].rearrange("p (t n) -> p t n", t=TT)
                link(tt(el[:, :, :], lp[:, :, NG:], bc(rbias[:, NG:], 1, TT), ALU.add))
                link(tt(gl[:, :, 0:NG], lp[:, :, 0:NG], bc(rbias[:, 0:NG], 1, TT), ALU.add))
                for t in range(TT):
                    link(ve.max(gmx[:, t, :], gl[:, t, :]))
                    link(ve.max_index(gix[:, t, :], gmx[:, t, :], gl[:, t, :]))
                link(ve.tensor_copy(gf[:, :], gix[:, :, 0]))
                for t in range(TT):
                    link(ts(oh[:, t, :], iota_e[:, 0:NG], gf[:, t:t + 1], None, ALU.is_equal))
                link(tt(eo[:, :, :].rearrange("p t (g e) -> p t g e", g=NG),
                        el[:, :, :].rearrange("p t (g e) -> p t g e", g=NG), bc(oh[:, :, :], 3, EG), ALU.mult))
                for t in range(TT):
                    link(ve.tensor_reduce(ch[:, t, :], eo[:, t, :].rearrange("p (g e) -> p e g", g=NG), AX.X, ALU.add))
                for t in range(TT):
                    link(ve.max(emx[:, t, :], ch[:, t, :]))
                    link(ve.max_index(eix[:, t, :], emx[:, t, :], ch[:, t, :]))
                for j in range(2):
                    link(ve.tensor_copy(ef[:, j, :], eix[:, :, j]))
                    link(stt(eid[:, j, :], gf[:, :], float(EG), ef[:, j, :], ALU.mult, ALU.add))
                link(ts(ngm[:, :], gmx[:, :, 0], -1.0, None, ALU.mult))
                tt(dlt[:, :], emx[:, :, 1], emx[:, :, 0], ALU.subtract).then_inc(S("top_ready"), 1)
                for j in range(2):
                    for t in range(TT):
                        link(ts(eq[:, j, t, :], iota_e[:, :], eid[:, j, t:t + 1], None, ALU.is_equal))
                tt(msk[:, :, :], eq[:, 0], eq[:, 1], ALU.add).then_inc(S("msk_ready"), 1)
                ve.wait_ge(S("pos_done"), i + 1)
                link(ve.tensor_copy(pos[:, :, :], PS[:, 0, 0:TT * NE].rearrange("p (t n) -> p t n", t=TT)))
                for j in range(2):
                    link(tt(ptmp[:, j], eq[:, j], pos[:, :, :], ALU.mult))
                    link(ve.tensor_reduce(pch[:, j, :], ptmp[:, j], AX.X, ALU.add))
                link(stt(v2[:, :, :], eid[:, :, :], float(CAP), pch[:, :, :], ALU.mult, ALU.add))
                for r in range(1, T // CAP):
                    dst = pr1[:, :, :] if r == 1 else val[:, :, :]
                    link(ts(dst, pch[:, :, :], float(r * CAP), float((NE - 1) * CAP), ALU.is_ge, ALU.mult))
                    link(tt(v2[:, :, :] if r < T // CAP - 1 else slot[:, :, :], v2[:, :, :], dst, ALU.add))
                ve.tensor_reduce(past[:, :], pr1[:, :, :], AX.XY, ALU.add).then_inc(S("past_ready"), 1)
                ve.wait_ge(S("past_ready"), i + 1)

            def token_weights(i):
                ve.wait_ge(S("gex_ready"), i + 1)
                link(stt(den[:, :], e21[:, :], 1.0, gsum[:, :], ALU.add, ALU.mult))
                link(ve.reciprocal(wgt[:, 0, :], den[:, :]))
                link(tt(wgt[:, 1, :], e21[:, :], wgt[:, 0, :], ALU.mult))
                for t in range(TT):
                    link(ts(wtok[:, t, :], eq[:, 0, t, :], wgt[:, 0, t:t + 1], None, ALU.mult))
                    link(stt(wtok[:, t, :], eq[:, 1, t, :], wgt[:, 1, t:t + 1], wtok[:, t, :], ALU.mult, ALU.add))

            def select(i, q):
                n = NSTEP_SEL * i + q
                if isinstance(q, int) and q < 2:
                    if (i, q) != (0, 0):
                        ve.wait_ge(S("m_written"), M_BASE * i + q * M_FIRST)
                else:
                    ve.wait_ge(S("m_written"), use(i, q - 2, SELT_AT) + 1)
                for t in range(TT):
                    ts(sel[:, t, :], iota_slot[:, :], slot[:, 0, t:t + 1], None, ALU.is_equal)\
                        .then_inc(S("sel_own"), 1)
                for t in range(TT):
                    ve.wait_ge(S("sel_own"), n * 5 + t + 1)
                    stt(sel[:, t, :], iota_slot[:, :], slot[:, 1, t:t + 1], sel[:, t, :].bitcast(F32), ALU.is_equal,
                        ALU.add).then_inc(S("sel_own"), 1)
                ve.wait_ge(S("sel_own"), n * 5 + 4)
                ts(slot[:, :, :], slot[:, :, :], -float(GS), None, ALU.add).then_inc(S("sel_own"), 1)
                ve.wait_ge(S("sel_own"), n * 5 + 5)

            def chunk(i, g, jj, c):
                n = 4 * NE * i + 4 * GE * g + 4 * jj + c
                s = items[moe_item[i] + jj % GE][0]
                ve.wait_ge(S("hi_ready"), n + 1)
                r = ring[s][:, 0:4096].rearrange("p (u n) -> p u n", u=2)[:, :, 512 * c:512 * c + 512]
                tt(wlo[:, c].rearrange("p k (u f) -> p u k f", u=2), r.rearrange("p u (k f) -> p u k f", k=2),
                   whi[:, c].bitcast(F32).rearrange("p k (u f) -> p u k f", u=2), ALU.subtract)\
                    .then_inc(S("lo_ready"), 1)

            def gather_sum(i, e):
                ve.wait_ge(S("flo_ready"), NE * i + e + 1)
                tt(gu[:, :], PS[0:64, 0, :], gu[:, :], ALU.add).then_inc(S("gu_ready"), 1)

            def gate(i, g, par, jj):
                n = NE * i + GE * g + jj
                ve.wait_ge(S("silu_ready"), n + 1)
                ve.wait_ge(S("gu_ready"), n + 1)
                if jj % GE == 0:
                    ve.wait_ge(S("m_evicted"), WSLOT_M(i, g, jj))
                stt(act[:, :], act[:, :], wslot[0:64, (par + jj // GE) % 2, jj % GE:jj % GE + 1], gu[:, FF:2 * FF],
                    ALU.mult, ALU.mult).then_inc(S("act_ready"), 1)

            def step(i, g, par, j, last):
                e = g * GE + j
                more = not (last and j >= 2)
                nxt = not (last and j == 3)
                if more:
                    chunk(i, g, j + 2, 0)
                    chunk(i, g, j + 2, 1)
                if nxt:
                    gather_sum(i, e + 1)
                if more:
                    chunk(i, g, j + 2, 2)
                if nxt:
                    gate(i, g, par, j + 1)
                if more:
                    chunk(i, g, j + 2, 3)
                if j == 3 and not last:
                    select(i, g + 2)
                if j % 2:
                    pair = g * 2 + j // 2 + NE // 2 * i
                    for n in range(2):
                        ve.wait_ge(S("ohi_ready"), pair * 2 + n + 1)
                        cs = slice(512 * n, 512 * n + 512)
                        tt(olo[:, cs], PS[:, 2 + n, :], ohi[:, cs].bitcast(F32), ALU.subtract)\
                            .then_inc(S("olo_ready"), 1)

            def moe(i):
                norm_scale(1 + 3 * i)
                norm_evict(1 + 3 * i, hT)
                for t in range(TT):
                    ve.tensor_copy(hhi[:, t, :], h[:, t, :]).then_inc(S("hhi_ready"), 1)
                for t in range(TT):
                    ve.wait_ge(S("hhi_ready"), TT * i + t + 1)
                    tt(hlo[:, t, :], h[:, t, :], hhi[:, t, :].bitcast(F32), ALU.subtract).then_inc(S("hlo_ready"), 1)
                route(i)
                if i == 0:
                    for b in range(2):
                        ve.memset(actT[:, b, :, CAP * (1 - b):CAP * (1 - b) + CAP], 0.0)
                select(i, 0)
                token_weights(i)
                for c in range(4):
                    chunk(i, 0, 0, c)
                select(i, 1)
                ve.wait_ge(S("past_done"), i + 1)
                ts(many[:, :], PS[0:1, 3, 0:1], 1.0, None, ALU.min).then_inc(S("many_ready"), 1)
                chunk(i, 0, 1, 0)
                chunk(i, 0, 1, 1)
                gather_sum(i, 0)
                chunk(i, 0, 1, 2)
                gate(i, 0, 0, 0)
                chunk(i, 0, 1, 3)
                for j in range(GE):
                    step(i, 0, 0, j, False)
                with ve.Fori(0, (NSTEP - 2) // 2) as r:
                    for sub in (1, 2):
                        for j in range(GE):
                            step(i, r * 2 + sub, sub % 2, j, False)
                for j in range(GE):
                    step(i, NSTEP - 1, 1, j, True)
                ve.wait_ge(S("comb_done"), NE // 2 * (i + 1))
                for t in range(TT):
                    for c in range(2):
                        xs = x[:, t, 512 * c:512 * c + 512]
                        ins = tt(xs, xs, PS[:, 4 + 2 * t + c, :], ALU.add)
                ins.then_inc(S("x_summed"), 1)
                ve.wait_ge(S("x_summed"), i + 1)

                def more(n):
                    name = lambda what: S(f"ov_{what}{i}")
                    for j in range(2):
                        for t in range(TT):
                            if j == 0:
                                ts(oh_ov[:, t, :], iota_slot[:, 0:CAP], slot[:, 0, t:t + 1], None, ALU.is_equal)\
                                    .then_inc(name("own"), 1)
                            else:
                                stt(oh_ov[:, t, :], iota_slot[:, 0:CAP], slot[:, 1, t:t + 1], oh_ov[:, t, :],
                                    ALU.is_equal, ALU.add).then_inc(name("own"), 1)
                        ve.wait_ge(name("own"), n * 5 + 2 * j + 2)
                    ts(slot[:, :, :], slot[:, :, :], -float(CAP), None, ALU.add).then_inc(name("own"), 1)
                    ve.wait_ge(name("own"), n * 5 + 5)
                    ve.wait_ge(name("gathered"), n + 1)
                    ve.tensor_copy(xo[:, :, :].rearrange("p k j -> p (k j)"), PS[:, 0, :])
                    ve.tensor_copy(selTo[:, :], PS[0:CAP, 1, 0:T])
                    ve.tensor_copy(wso[:, :], PS[0:CAP, 1, T:T + 1]).then_inc(name("x"), 1)
                    ve.wait_ge(name("x"), n + 1)
                    ve.wait_ge(name("silu"), n + 1)
                    stt(acto[:, :], slu[:, :], wso[:, 0:1], PS[0:CAP, 2, FF:2 * FF], ALU.mult, ALU.mult)\
                        .then_inc(name("act"), 1)
                    ve.wait_ge(name("actT"), n + 1)
                    ve.tensor_copy(actTo[:, :, :].rearrange("p k j -> p (k j)"), PS[:, 3, 0:2 * CAP])\
                        .then_inc(name("actTr"), 1)
                    ve.wait_ge(name("free"), n + 2)
                    ve.tensor_copy(oo[:, :].rearrange("p (b n) -> p b n", b=2), PS[0:CAP, 0:2, :]).then_inc(name("o"), 1)
                    ve.wait_ge(name("comb"), n + 1)
                    for t in range(TT):
                        for c in range(2):
                            xs = x[:, t, 512 * c:512 * c + 512]
                            ins = tt(xs, xs, PS[:, 4 + 2 * t + c, :], ALU.add)
                    ins.then_inc(name("added"), 1)
                    ve.wait_ge(name("added"), n + 1)

                link(ts(slot[:, :, :], slot[:, :, :], float(GS), None, ALU.add))
                overflow(ve, i, more)
                ve.sem_inc(S("x_ready"), 1)

            def ple(i):
                dense_lo(IT["ple"][i][0], 0, 2)
                norm_scale(2 + 3 * i)
                dense_lo(IT["ple"][i][0], 2, 4)
                split_evict(2 + 3 * i)
                dense_lo(IT["ple"][i][2], 0, 4)
                for n in range(4):
                    k = 4 * i + n
                    c, t = divmod(n, 2)
                    b = n % 2
                    ve.wait_ge(S("sg_ready"), k + 1)
                    link(tt(sg[b][:, :], sg[b][:, :], PS[:, n, :], ALU.mult))
                    xs = x[:, t, 512 * c:512 * c + 512]
                    ins = tt(xs, xs, sg[b][:, :], ALU.add)
                    ins.then_inc(S("ple_used"), 1)
                    ve.wait_ge(S("ple_used"), k + 1)
                if i == 0:
                    ve.sem_inc(S("x_ready"), 1)

            moe(0)
            ple(0)

            norm_scale(3)
            split_evict(3)

            def qkv_evict(w):
                n = 2 * w + 1
                ve.wait_ge(S("split_done"), 4 * dense.index(IT["qkv"][w]) + 4)
                dst = qk[:, 1, 8 * w:8 * w + 8, :].rearrange("p a d -> p (a d)") if w < 4 else \
                    vt[:, 1, 512 * (w - 4):512 * (w - 4) + 512]
                ve.tensor_copy(dst, PS[:, n % 4, :]).then_inc(S("qkv_d"), 1)

            for w in range(6):
                dense_lo(IT["qkv"][w], 0, 4)
                if w:
                    qkv_evict(w - 1)
            for t in range(TT):
                ve.wait_ge(S("sq_ready"), t + 1)
                ve.tensor_reduce(qss[:, t, :], sq[:, :, :], AX.X, ALU.add).then_inc(S("qss_ready"), 1)
                ve.wait_ge(S("qss_ready"), t + 1)
                ts(qms[:, t, :], qss[:, t, :], 1.0 / HD, EPS, ALU.mult, ALU.add).then_inc(S("qms_ready"), 1)
            qkv_evict(5)
            for t in range(TT):
                ve.wait_ge(S("qrs_ready"), t + 1)
                tt(qk[:, t], qk[:, t], bc(qrs[:, t, :], 2, HD), ALU.mult).then_inc(S("qkn_ready"), 1)
            ve.wait_ge(S("qkw_loaded"), 64)
            for t in range(TT):
                for n in range(2):
                    ve.wait_ge(S("k_T"), 2 * t + n + 1)
                    ts(kT[:, 4 * n:4 * n + 4, P * t:P * t + P], PS[:, 6 + n, :].rearrange("p (a t) -> p a t", a=4),
                       qkw[:, 1:2], None, ALU.mult).then_inc(S("kT_ready"), 1)

            def scores(a):
                b = a % 4
                ve.wait_ge(S("bias_ready"), a + 1)
                ve.wait_ge(S("s_done"), a + 1)
                if a >= 4:
                    ve.wait_ge(S("prob_T"), a - 3)
                bi_ = bias[a // (NH // 2)][:, a % (NH // 2)].rearrange("p t r c -> p (t r) c")
                tt(prob[:, b].rearrange("p t (r c) -> p (t r) c", r=ROWS),
                   PS[:, SB[a % 3], :].rearrange("p (r c) -> p r c", c=GW), bi_[:, :, ::-1], ALU.add)\
                    .then_inc(S("sb_ready"), 1)
                ve.wait_ge(S("sb_ready"), a + 1)
                ve.tensor_reduce(mx[:, b, :], prob[:, b], AX.X, ALU.max, negate=True).then_inc(S("mx_ready"), 1)

            def normalise(a):
                b = a % 4
                ve.wait_ge(S("exp_ready"), TT * (a + 1))
                link(ve.reciprocal(rr[:, b, :], rs[:, b, :]))
                for t in range(TT):
                    ts(prob[:, b, t, :], prob[:, b, t, :], rr[:, b, t:t + 1], None, ALU.mult)\
                        .then_inc(S("prob_ready"), 1)

            def out_evict(a):
                ve.wait_ge(S("pv_done"), a + 2)
                ve.tensor_copy(oT[:, a // 2, :], PS[:, 4 + (a // 2) % 2, 0:T]).then_inc(S("oT_ready"), 1)

            for a in range(NH + 4):
                if a < NH:
                    scores(a)
                if 1 <= a <= NH:
                    normalise(a - 1)
                if a >= 5 and a % 2 == 1:
                    out_evict(a - 5)
            for n in range(4):
                c, t = divmod(n, 2)
                ve.wait_ge(S("wo_done"), n + 1)
                xs = x[:, t, 512 * c:512 * c + 512]
                ins = tt(xs, xs, PS[:, 6 + n % 2, :], ALU.add)
                ins.then_inc(S("wo_used"), 1)
            ve.wait_ge(S("wo_used"), 4)
            ve.sem_inc(S("x_ready"), 1)
            moe(1)
            ple(1)

        @block.tensor
        def _(pe):
            mm = pe.matmul

            def norm_T(n):
                for t in range(TT):
                    pe.wait_ge(S("h_ready"), TT * n + t + 1)
                    for kq in range(2):
                        for k in range(4):
                            ins = pe.transpose(PS[:, NB + 2 * t + kq, P * k:P * k + P], h[:, t, 4 * kq + k::KD],
                                               ident[:, :])
                        ins.then_inc(S("h_T2") if t else S("h_T"), 1)
                if n in PLAIN:
                    pe.wait_ge(S("hT_a"), 2 * PLAIN[n] + 2)
                    pe.wait_ge(S("hT_d"), 2 * PLAIN[n] + 2)
                else:
                    pe.wait_ge(S("hTl_ready"), 4 * SPLIT[n] + 4)

            def dense_mm(n, b0):
                q = 4 * dense.index(n)
                for c in range(4):
                    pe.wait_ge(S("dense_lo"), q + c + 1)
                    for k in range(2):
                        for t in range(TT):
                            r = slice(P * t, P * t + P)
                            lo = dense_w(n, c)[1][:, k, :]
                            for w, (a_, b_) in enumerate(((hTh, lo), (hTl, dwh[:, c, k, :]), (hTh, dwh[:, c, k, :]))):
                                ins = mm(PS[:, b0 + t, :], a_[:, 2 * c + k, r], b_, start=(c, k, w) == (0, 0, 0),
                                         stop=(c, k, w) == (3, 1, 2))
                    ins.then_inc(S("split_done"), 1)

            pe.wait_ge(S("ident_ready"), 1)
            pe.wait_ge(S("coef_ready"), 1)
            for n, q in enumerate((0, 2, 11, 12)):
                ins = pe.transpose(PS[:, 0, SG * n:SG * n + SG], pq[:, q], ident[0:SG, 0:SG])
            ins.then_inc(S("prm_T"), 1)
            pe.wait_ge(S("c_loaded"), 64)
            for c in range(2):
                for a in range(4):
                    ins = pe.transpose(PS[:, 1 + c, P * a:P * a + P],
                                       craw[:, c, a].rearrange("p d n -> p (d n)"), ident[:, :])
                ins.then_inc(S("c_T"), 1)
            norm_T(0)
            arrived(pe, IT["w_in"])
            w_in = ring[0][:, 0:KD * SW].rearrange("p (k n) -> p k n", k=KD)
            for a in range(4):
                for k in range(KD):
                    ins = mm(PS[:, 4 + a // 2, T * (a % 2):T * (a % 2) + T], w_in[:, k, P * a:P * a + P],
                             s5hT[:, k, :], start=k == 0, stop=k == KD - 1)
            ins.then_inc(S("u_done"), 1)
            pe.wait_ge(S("u_done"), 1)
            for n in range(SG // 2):
                pe.wait_ge(S("s5W_re"), n // (SG // 4) + 1)
                pe.wait_ge(S(f"s5W_im{n // (SG // 4)}"), 1)
                if n >= 2:
                    pe.wait_ge(S("WT_ready"), n - 1)
                else:
                    pe.wait_ge(S("cT_ready"), 2)
                for gg in range(2):
                    for c in range(2):
                        o_ = 256 * gg + 128 * c
                        ins = pe.transpose(PS[:, 2 + n % 2, o_:o_ + P],
                                           s5W[:, c, 2 * n + gg].rearrange("p l h -> p (l h)"), ident[:, :])
                ins.then_inc(S("W_T"), 1)
            pe.wait_ge(S("us_loaded"), 16 * L)
            pe.wait_ge(S("WT_ready"), SG // 2)
            pe.wait_ge(S("uT_half"), 2)
            for c in range(2):
                for g in range(SG):
                    ins = mm(PS[:, 4 + 2 * c + g // 16, NC_ * (g % 16):NC_ * (g % 16) + NC_], s5WT[:, c, g, :],
                             us[:, g, :], start=True, stop=True)
            ins.then_inc(S("v_done"), 1)
            for n in range(SG // 4):
                pe.wait_ge(S("s5V_re"), n // (SG // 8) + 1)
                pe.wait_ge(S("s5V_im"), n // (SG // 8) + 1)
                if n >= 2:
                    pe.wait_ge(S("s5T_ready"), n - 1)
                if n == 1:
                    pe.wait_ge(S("WT_ready"), SG // 2)
                for gg in range(4):
                    for c in range(2):
                        for d in range(2):
                            hf = slice(64 * d, 64 * d + 64)
                            ins = mm(PS[:, 2 * (n % 2) + d, P * gg:P * gg + P],
                                     s5W[hf, c, 4 * n + gg].rearrange("p l h -> p (l h)"),
                                     s5V[hf, c, 4 * n + gg].rearrange("p l h -> p (l h)"), start=c == 0, stop=c == 1)
                            if (gg, c) == (3, 1):
                                ins.then_inc(S("T_done"), 1)
            pe.wait_ge(S("s5T_ready"), SG // 4)
            pe.wait_ge(S("S_ready"), 2)
            def chunk_outputs(k):
                if k >= 2:
                    pe.wait_ge(S("ys_part"), k - 1)
                for g in range(8 * k, 8 * k + 8):
                    o_ = PS[0:NC_, 2 * (k % 2) + g % 8 // 4, P * (g % 4):P * (g % 4) + P]
                    mm(o_, us[:, g, :], s5T[:, g, :], start=True, stop=False)
                    mm(o_, sc[0][:, g, :], s5V[:, 0, g].rearrange("p l h -> p (l h)"), start=False, stop=False)
                    ins = mm(o_, sc[1][:, g, :], s5V[:, 1, g].rearrange("p l h -> p (l h)"), start=False, stop=True)
                ins.then_inc(S("y_done"), 1)

            def outputs_T(k):
                pe.wait_ge(S("ys_part"), k + 1)
                for s in range(L):
                    ins = pe.transpose(PS[:, 4 + k, NC_ * s:NC_ * s + NC_],
                                       ys[k % 2][:, s].rearrange("c g h -> c (g h)"), ident[0:NC_, 0:NC_])
                ins.then_inc(S("y_T"), 1)

            for k in range(5):
                if k < 4:
                    chunk_outputs(k)
                if k:
                    outputs_T(k - 1)
            arrived(pe, IT["w_out"][0])
            arrived(pe, IT["w_out"][1])
            for n in range(4):
                t, c = divmod(n, 2)
                if n >= 2:
                    pe.wait_ge(S("glu_used"), n - 1)
                for w in range(2):
                    wv = ring[w][:, 0:4 * D].rearrange("p (k n) -> p k n", k=4)
                    for k in range(4):
                        if (n, w) == (0, 0):
                            pe.wait_ge(S("gelu_ready"), k + 1)
                        ins = mm(PS[:, 4 + 2 * (n % 2) + w, :], yT[4][:, k, P * t:P * t + P],
                                 wv[:, k, 512 * c:512 * c + 512], start=k == 0, stop=k == 3)
                ins.then_inc(S("glu_done"), 1)

            def gather_up(i, g, par, jj, c0, c1):
                n = NE * i + GE * g + jj
                if c0 == 0 and not (isinstance(n, int) and n == 0):
                    pe.wait_ge(S("gu_ready"), n)
                p_ = (par + jj // GE) % 2
                for c in range(c0, c1):
                    pe.wait_ge(S("lo_ready"), n * 4 + c + 1)
                    for k in range(2):
                        for w, w_half in enumerate((wlo, whi)):
                            ins = mm(PS[:, 0, :], xg[:, p_, jj % GE, 2 * c + k].rearrange("p c j -> p (c j)"),
                                     w_half[:, c, k, :], start=(c, k, w) == (0, 0, 0), stop=(c, k, w) == (3, 1, 1))
                    ins.then_inc(S("split_used"), 1)

            def bank1(m):
                if not (isinstance(m, int) and m == 0):
                    pe.wait_ge(S("m_evicted"), m)

            def units(i, g, par, lst, m):
                for n, u in enumerate(lst):
                    b = 1
                    if lst is ALL_UNITS:
                        b = FIRST_BANKS[n % len(FIRST_BANKS)]
                        if n >= len(FIRST_BANKS):
                            pe.wait_ge(S("m_evicted"), m + n - len(FIRST_BANKS) + 1)
                    else:
                        bank1(m + n)
                    if lst is ALL_UNITS and n == 0 or lst is not ALL_UNITS and u == 0:
                        pe.wait_ge(S("sel_own"), (NSTEP_SEL * i + g) * 5 + 4)
                    if u == "selT":
                        for pr_ in range(2):
                            for t in range(TT):
                                ins = pe.transpose(PS[:, b, T * pr_ + P * t:T * pr_ + P * t + P],
                                                   sel[:, t, P * pr_:P * pr_ + P].bitcast(F32), ident[:, :])
                    elif u == "weights":
                        if lst is ALL_UNITS:
                            pe.wait_ge(S("lo_ready"), 4 * NE * i + 1)
                        for e in range(GE):
                            for t in range(TT):
                                ins = mm(PS[0:64, b, e:e + 1], sel[:, t, CAP * e:CAP * e + CAP].bitcast(F32),
                                         wtok[:, t, bass.ds(g * GE + e, 1)], start=t == 0, stop=t == 1)
                    else:
                        for c, h_half in enumerate((hhi, hlo)):
                            for t in range(TT):
                                ins = mm(PS[:, b, GS * c:GS * c + GS], h_half[:, t, u::KD], sel[:, t, :],
                                         start=t == 0, stop=t == 1)
                    ins.then_inc(S("m_written"), 1)

            def down(i, g, j, n, s):
                b = j % 2
                wd = ring[s][:, 4096:6144].rearrange("p (k n) -> p k n", k=2)
                for k in range(2):
                    ins = mm(PS[:, 2 + n, :], actT[:, b, k, :], wd[:, k, 512 * n:512 * n + 512],
                             start=(b, k) == (0, 0), stop=(b, k) == (1, 1))
                return ins

            def combine(i, pair, spar, pr_, first, last):
                for n in range(2):
                    pe.wait_ge(S("olo_ready"), pair * 2 + n + 1)
                    for t in range(TT):
                        for w, o_half in enumerate((ohi, olo)):
                            ins = mm(PS[:, 4 + 2 * t + n, :], selT[:, spar, pr_, P * t:P * t + P],
                                     o_half[:, 512 * n:512 * n + 512], start=first and w == 0, stop=last and w == 1)
                ins.then_inc(S("comb_done"), 1)

            def step(i, g, par, j, last):
                e = NE * i + GE * g + j
                off = j if last else M_POS[j][0]
                mt = use(i, g, off)
                s = items[moe_item[i] + j][0]

                def part(n):
                    if not last:
                        units(i, g + 1, 1 - par, UNITS[j][n], use(i, g, M_POS[j][n + 1]))

                pe.wait_ge(S("act_ready"), e + 1)
                bank1(mt)
                for k in range(2):
                    ins = mm(PS[:, 1, CAP * k:CAP * k + CAP], act[:, k::2], ident[0:CAP, 0:CAP], start=True, stop=True)
                ins.then_inc(S("m_written"), 1)
                if not (last and j == 3):
                    gather_up(i, g, par, j + 1, 0, 2)
                    part(0)
                    gather_up(i, g, par, j + 1, 2, 4)
                    part(1)
                if j % 2 == 0:
                    pair = NE // 2 * i + g * 2 + j // 2 - 1
                    if not (isinstance(g, int) and g == 0 and j == 0):
                        first = isinstance(g, int) and g == 0 and j == 2
                        combine(i, pair, (par - (j == 0)) % 2, 1 - j // 2, first, False)
                pe.wait_ge(S("m_evicted"), mt + 1)
                if j % 2 == 0:
                    pair = NE // 2 * i + g * 2 + j // 2
                    if not (isinstance(pair, int) and pair == 0):
                        pe.wait_ge(S("olo_ready"), pair * 2)
                down(i, g, j, 0, s)
                part(2)
                down(i, g, j, 1, s).then_inc(S("d_done"), 1)

            def moe(i):
                norm_T(1 + 3 * i)
                pe.wait_ge(S("router_loaded"), 64 * (i + 1))
                for t in range(TT):
                    for k in range(KD):
                        ins = mm(PS[:, 0, (NG + NE) * t:(NG + NE) * (t + 1)], hT[:, k, P * t:P * t + P], wr[:, k, :],
                                 start=k == 0, stop=k == KD - 1)
                ins.then_inc(S("logits_done"), 1)
                pe.wait_ge(S("msk_ready"), i + 1)
                mm(PS[:, 0, 0:NE], tri[:, :], msk[:, 0], start=True, stop=True)
                mm(PS[:, 0, NE:2 * NE], ones[:, :], msk[:, 0], start=True, stop=False)
                mm(PS[:, 0, NE:2 * NE], tri[:, :], msk[:, 1], start=False, stop=True).then_inc(S("pos_done"), 1)
                pe.wait_ge(S("hhi_ready"), TT * (i + 1))
                pe.wait_ge(S("hlo_ready"), TT * (i + 1))
                units(i, 0, 0, ALL_UNITS, M_BASE * i)
                pe.wait_ge(S("m_evicted"), M_BASE * i + M_FIRST)
                pe.wait_ge(S("past_ready"), i + 1)
                mm(PS[0:1, 3, 0:1], past[:, :], ones[:, 0:1], start=True, stop=True).then_inc(S("past_done"), 1)
                gather_up(i, 0, 0, 0, 0, 4)
                for j in range(GE):
                    step(i, 0, 0, j, False)
                with pe.Fori(0, (NSTEP - 2) // 2) as r:
                    for sub in (1, 2):
                        for j in range(GE):
                            step(i, r * 2 + sub, sub % 2, j, False)
                for j in range(GE):
                    step(i, NSTEP - 1, 1, j, True)
                combine(i, NE // 2 * (i + 1) - 1, 1, 1, False, True)

                def more(n):
                    name = lambda what: S(f"ov_{what}{i}")
                    pe.wait_ge(name("own"), n * 5 + 5)
                    for k in range(KD):
                        for q, h_half in enumerate((hhi, hlo)):
                            for t in range(TT):
                                mm(PS[:, 0, CAP * k:CAP * k + CAP], h_half[:, t, k::KD].bitcast(F32), oh_ov[:, t, :],
                                   start=(q, t) == (0, 0), stop=(q, t) == (1, 1))
                    for t in range(TT):
                        mm(PS[0:CAP, 1, P * t:P * t + P], oh_ov[:, t, :], ident[:, :], start=True, stop=True)
                    for t in range(TT):
                        ins = mm(PS[0:CAP, 1, T:T + 1], oh_ov[:, t, :], wtok[:, t, bass.ds(n % NE, 1)],
                                 start=t == 0, stop=t == 1)
                    ins.then_inc(name("gathered"), 1)
                    s = items[moe_item[i]][0]
                    pe.wait_ge(S(f"ov_loaded{i}"), n * 48 + 48)
                    pe.wait_ge(name("x"), n + 1)
                    wv = ring[s][:, 0:4096].rearrange("p (u k f) -> p u k f", u=2, k=KD)
                    for u in range(2):
                        for k in range(KD):
                            ins = mm(PS[0:CAP, 2, FF * u:FF * u + FF], xo[:, k, :], wv[:, u, k, :],
                                     start=k == 0, stop=k == KD - 1)
                    ins.then_inc(name("gu"), 1)
                    pe.wait_ge(name("act"), n + 1)
                    for k in range(2):
                        ins = mm(PS[:, 3, CAP * k:CAP * k + CAP], acto[:, k::2], ident[0:CAP, 0:CAP],
                                 start=True, stop=True)
                    ins.then_inc(name("actT"), 1)
                    pe.wait_ge(name("actTr"), n + 1)
                    wd = ring[s][:, 4096:6144].rearrange("p (k n) -> p k n", k=2)
                    for c in range(2):
                        for k in range(2):
                            ins = mm(PS[0:CAP, c, :], actTo[:, k, :], wd[:, k, 512 * c:512 * c + 512],
                                     start=k == 0, stop=k == 1)
                    ins.then_inc(name("free"), 1)
                    pe.wait_ge(name("o"), n + 1)
                    for t in range(TT):
                        for c in range(2):
                            ins = mm(PS[:, 4 + 2 * t + c, :], selTo[:, P * t:P * t + P], oo[:, 512 * c:512 * c + 512],
                                     start=True, stop=True)
                    ins.then_inc(name("comb"), 1)

                overflow(pe, i, more)

            def ple(i):
                ga, pj, gb = IT["ple"][i]
                sp_ = items[pj][0]
                arrived(pe, pj)
                pv = ring[sp_][:, 2048:2560].rearrange("p (t n) -> p t n", t=TT)
                for k in range(2):
                    for t in range(TT):
                        ins = pe.transpose(PS[:, 0, T * k + P * t:T * k + P * t + P], pv[:, t, k::2], ident[:, :])
                ins.then_inc(S("p_T"), 1)
                pe.wait_ge(S("pT_ready"), i + 1)
                wp_v = ring[sp_][:, 0:2048].rearrange("p (k n) -> p k n", k=2)
                for n in range(4):
                    c, t = divmod(n, 2)
                    for k in range(2):
                        mm(PS[:, n, :], pT[:, k, P * t:P * t + P], wp_v[:, k, 512 * c:512 * c + 512],
                           start=k == 0, stop=k == 1)
                norm_T(2 + 3 * i)
                dense_mm(ga, 4)
                dense_mm(gb, 6)

            moe(0)
            ple(0)

            norm_T(3)
            for w in range(6):
                if w >= 2:
                    pe.wait_ge(S("qkv_a"), w - 1)
                    pe.wait_ge(S("qkv_d"), w - 1)
                dense_mm(IT["qkv"][w], 2 * (w % 2))
            for t in range(TT):
                pe.wait_ge(S("qkn_ready"), t + 1)
                for b, what in ((4, "q_T"), (6, "k_T")):
                    for n in range(2):
                        if t:
                            pe.wait_ge(S("qT_ready") if b == 4 else S("kT_ready"), n + 1)
                        for a in range(4):
                            hd = (0 if b == 4 else NH) + 2 * (4 * n + a)
                            ins = pe.transpose(PS[:, b + n, P * a:P * a + P],
                                               qk[:, t, hd:hd + 2, :].rearrange("p a d -> p (a d)"), ident[:, :])
                        ins.then_inc(S(what), 1)
            pe.wait_ge(S("qT_ready"), 4)
            pe.wait_ge(S("kT_ready"), 4)
            pe.wait_ge(S("qkv_a"), 6)
            pe.wait_ge(S("qkv_d"), 6)

            def scores(a):
                if a >= 3:
                    pe.wait_ge(S("sb_ready"), a - 2)
                r = slice(64 * (a % 2), 64 * (a % 2) + 64)
                for t in range(TT):
                    ins = mm(PS[:, SB[a % 3], T * t:T * t + T], qT[r, a // 2, P * t:P * t + P], kT[r, a // 2, :],
                             start=True, stop=True)
                ins.then_inc(S("s_done"), 1)

            def prob_T(a):
                pe.wait_ge(S("prob_ready"), TT * (a + 1))
                if a >= 2:
                    pe.wait_ge(S("probT_ready"), a - 1)
                for kt in range(2):
                    for t in range(TT):
                        ins = pe.transpose(PS[:, 2 + a % 2, T * kt + P * t:T * kt + P * t + P],
                                           prob[:, a % 4, t, P * kt:P * kt + P], ident[:, :])
                ins.then_inc(S("prob_T"), 1)

            def values(a):
                pe.wait_ge(S("probT_ready"), a + 1)
                if a >= 4 and a % 2 == 0:
                    pe.wait_ge(S("oT_ready"), a // 2 - 1)
                r = slice(64 * (a % 2), 64 * (a % 2) + 64)
                for kt in range(2):
                    ins = mm(PS[r, 4 + (a // 2) % 2, 0:T], vt[:, kt, HD * a:HD * a + HD], probT[:, a % 2, kt, :],
                             start=kt == 0, stop=kt == 1)
                ins.then_inc(S("pv_done"), 1)

            for a in range(NH + 3):
                if a < NH:
                    scores(a)
                if 2 <= a < NH + 2:
                    prob_T(a - 2)
                if a >= 3:
                    values(a - 3)
            pe.wait_ge(S("oT_ready"), NH // 2)
            for n in range(4):
                c, t = divmod(n, 2)
                if t == 0:
                    arrived(pe, IT["wo"][c])
                if n >= 2:
                    pe.wait_ge(S("wo_used"), n - 1)
                wv = ring[items[IT["wo"][c]][0]][:, 0:4096].rearrange("p (k n) -> p k n", k=KD)
                for k in range(KD):
                    ins = mm(PS[:, 6 + n % 2, :], oT[:, k, P * t:P * t + P], wv[:, k, :], start=k == 0, stop=k == KD - 1)
                ins.then_inc(S("wo_done"), 1)
            moe(1)
            ple(1)


_INS = ["x", "p", "norm_mix", "norm_ffn", "norm_ple", "s5_w_in", "s5_lam_re", "s5_lam_im", "s5_log_dt",
        "s5_b_re", "s5_b_im", "s5_c_re", "s5_c_im", "s5_d", "s5_w_out", "nat_w_qkv", "nat_q_norm", "nat_k_norm",
        "nat_rpb", "nat_w_o", "moe_w_group", "moe_b_group", "moe_w_expert", "moe_b_expert", "moe_w_gate",
        "moe_w_up", "moe_w_down", "ple_w_proj", "ple_w_gate"]


def kernel(**inputs):
    import numpy as np
    import concourse.bacc as bacc
    from concourse.bass_utils import run_bass_kernel_spmd

    nc = bacc.Bacc("TRN2", target_bir_lowering=False, num_devices=1)
    arrays, views = {}, {}
    for name in _INS:
        a = np.ascontiguousarray(inputs[name])
        arrays[f"in_{name}"] = a
        views[name] = nc.dram_tensor(f"in_{name}", a.shape, mybir.dt.from_np(a.dtype), kind="ExternalInput").ap()
    out = nc.dram_tensor("out_0", (1, T, D), F32, kind="ExternalOutput").ap()
    program(nc, views, out)
    r = run_bass_kernel_spmd(nc, [arrays], core_ids=[0])
    return r.results[0]["out_0"]
```
